# Optimizing a Trainium2 kernel written in Bass

```python
import jax, jax.numpy as jnp
from jax import lax
import numpy as np
import math

D_MODEL = 1024
BATCH = 1
SEQ = 256
DEPTH = 2

CTX_LEN = 256
GRID_W = 64
EPS = 1e-6
ROPE_BASE = 10000.0
Q_BLOCK = 128

MLA_HEADS = 8
MLA_Q_RANK = 384
MLA_KV_RANK = 256
MLA_NOPE = 64
MLA_ROPE = 32
MLA_V = 64
MLA_SCALE = (MLA_NOPE + MLA_ROPE) ** -0.5

GLA_HEADS = 4
GLA_DK = 64
GLA_DV = 128
GLA_GATE_RANK = 16
GLA_GATE_TAU = 16.0
GLA_CHUNK = 64
GLA_QK_W = GLA_HEADS * GLA_DK
GLA_V_W = GLA_HEADS * GLA_DV

NA_HEADS = 8
NA_HEAD_DIM = 64
NA_KH = 8
NA_KW = 16
NA_W = NA_HEADS * NA_HEAD_DIM
NA_SCALE = NA_HEAD_DIM ** -0.5

FFN_HIDDEN = ((8 * D_MODEL + 3 * 256 - 1) // (3 * 256)) * 256

N_BRANCH = 3
MLA_OUT_W = MLA_HEADS * MLA_V
A_SPLITS = (MLA_Q_RANK, MLA_KV_RANK, MLA_ROPE)
B_SPLITS = (GLA_QK_W, GLA_QK_W, GLA_V_W, GLA_V_W, GLA_GATE_RANK, GLA_GATE_RANK)
C_SPLITS = (NA_W, NA_W, NA_W)
GROUP_SPLITS = (sum(A_SPLITS), sum(B_SPLITS), sum(C_SPLITS), N_BRANCH * D_MODEL)
IN_WIDTH = sum(GROUP_SPLITS)


def split_cols(z, sizes):
    idx = np.cumsum(sizes)[:-1].tolist()
    return jnp.split(z, idx, axis=-1)

def rms_norm(x, w):
    xf = x.astype(jnp.float32)
    y = xf * lax.rsqrt(jnp.mean(xf * xf, axis=-1, keepdims=True) + EPS)
    return (y * w.astype(jnp.float32)).astype(x.dtype)

def modulate(h, shift, scale):
    return h * (1 + scale) + shift

def to_heads(t, n_heads):
    b, l, w = t.shape
    return t.reshape(b, l, n_heads, w // n_heads).transpose(0, 2, 1, 3)

def from_heads(t):
    b, h, l, d = t.shape
    return t.transpose(0, 2, 1, 3).reshape(b, l, h * d)

def axial_rope_tables(length):
    t = jnp.arange(length)
    rows = (t // GRID_W).astype(jnp.float32)
    cols = (t % GRID_W).astype(jnp.float32)
    n_freq = MLA_ROPE // 4
    inv_freq = ROPE_BASE ** (-jnp.arange(n_freq, dtype=jnp.float32) / n_freq)
    ang = jnp.concatenate([rows[:, None] * inv_freq, cols[:, None] * inv_freq], axis=-1)
    return jnp.cos(ang), jnp.sin(ang)

def apply_rope(x, cos, sin):
    half = x.shape[-1] // 2
    x1, x2 = x[..., :half], x[..., half:]
    cos = cos.astype(x.dtype)
    sin = sin.astype(x.dtype)
    return jnp.concatenate([x1 * cos - x2 * sin, x1 * sin + x2 * cos], axis=-1)

def dense_attend(q, k, v):
    s = jnp.einsum('bhqd,bhkd->bhqk', q, k).astype(jnp.float32)
    p = jax.nn.softmax(s, axis=-1).astype(v.dtype)
    return jnp.einsum('bhqk,bhkd->bhqd', p, v)

def mla_queries(a, q_norm_w, w_q_up):
    q_down = a[..., :MLA_Q_RANK]
    q = to_heads(rms_norm(q_down, q_norm_w) @ w_q_up, MLA_HEADS)
    return q[..., :MLA_NOPE], q[..., MLA_NOPE:]

def mla_keys(a, kv_norm_w, w_kv_up):
    _, kv_down, k_rope = split_cols(a, A_SPLITS)
    kv = to_heads(rms_norm(kv_down, kv_norm_w) @ w_kv_up, MLA_HEADS)
    return kv[..., :MLA_NOPE], k_rope, kv[..., MLA_NOPE:]

def mla_attend(q_nope, q_rope, k_nope, k_rope, v):
    s = (jnp.einsum('bhqd,bhkd->bhqk', q_nope, k_nope)
         + jnp.einsum('bhqr,bkr->bhqk', q_rope, k_rope)).astype(jnp.float32) * MLA_SCALE
    p = jax.nn.softmax(s, axis=-1).astype(v.dtype)
    return jnp.einsum('bhqk,bhkd->bhqd', p, v)

def mla_mixer(a_lat, a_ctx, q_norm_w, kv_norm_w, w_q_up, w_kv_up, cos, sin, need_ctx_out):
    qn, qr = mla_queries(a_lat, q_norm_w, w_q_up)
    qr = apply_rope(qr, cos, sin)
    kn, kr, v = mla_keys(a_lat, kv_norm_w, w_kv_up)
    kr = apply_rope(kr, cos, sin)
    kn_c, kr_c, v_c = mla_keys(a_ctx, kv_norm_w, w_kv_up)
    kn_all = jnp.concatenate([kn, kn_c], axis=2)
    kr_all = jnp.concatenate([kr, kr_c], axis=1)
    v_all = jnp.concatenate([v, v_c], axis=2)
    b, h, l, _ = qn.shape
    nb = l // Q_BLOCK

    def blocks(t):
        return t.reshape(b, h, nb, Q_BLOCK, t.shape[-1]).transpose(2, 0, 1, 3, 4)

    o = lax.map(lambda qb: mla_attend(qb[0], qb[1], kn_all, kr_all, v_all), (blocks(qn), blocks(qr)))
    o = o.transpose(1, 2, 0, 3, 4).reshape(b, h, l, MLA_V)
    y_lat = from_heads(o)
    y_ctx = None
    if need_ctx_out:
        qn_c, qr_c = mla_queries(a_ctx, q_norm_w, w_q_up)
        y_ctx = from_heads(mla_attend(qn_c, qr_c, kn_c, kr_c, v_c))
    return y_lat, y_ctx

def gla_chunked(q, k, v, log_a, s0):
    b, h, l, _ = q.shape
    dv = v.shape[-1]
    n = l // GLA_CHUNK

    def ch(t):
        return t.reshape(b, h, n, GLA_CHUNK, t.shape[-1])

    q, k, v, log_a = ch(q), ch(k), ch(v), ch(log_a)
    cum = jnp.cumsum(log_a, axis=3)
    last = cum[:, :, :, -1:, :]
    q_dec = q * jnp.exp(cum)
    k_inv = k * jnp.exp(-cum)
    k_end = k * jnp.exp(last - cum)
    lower = jnp.tril(jnp.ones((GLA_CHUNK, GLA_CHUNK), dtype=bool))
    att = jnp.where(lower, jnp.einsum('bhncd,bhnsd->bhncs', q_dec, k_inv), 0.0)
    o_intra = jnp.einsum('bhncs,bhnse->bhnce', att, v)
    kv_chunk = jnp.einsum('bhncd,bhnce->bhnde', k_end, v)
    decay = jnp.exp(last[:, :, :, 0, :])

    def step(state, inp):
        dec, kv = inp
        return dec[..., None] * state + kv, state

    s_final, s_prev = lax.scan(step, s0, (jnp.moveaxis(decay, 2, 0), jnp.moveaxis(kv_chunk, 2, 0)))
    s_prev = jnp.moveaxis(s_prev, 0, 2)
    o_inter = jnp.einsum('bhncd,bhnde->bhnce', q_dec, s_prev)
    return (o_intra + o_inter).reshape(b, h, l, dv), s_final

def gla_bidir(q, k, v, la_f, la_b, s0_f, s0_b):
    o_f, s_f = gla_chunked(q, k, v, la_f, s0_f)
    flip = lambda t: jnp.flip(t, axis=2)
    o_b, s_b = gla_chunked(flip(q), flip(k), flip(v), flip(la_b), s0_b)
    return o_f + flip(o_b), s_f, s_b

def gla_log_decay(lr, w_up, b_up):
    z = (lr @ w_up + b_up).astype(jnp.float32)
    return to_heads(jax.nn.log_sigmoid(z) / GLA_GATE_TAU, GLA_HEADS)

def gla_mixer(b_lat, b_ctx, w_gate_f, b_gate_f, w_gate_b, b_gate_b, norm_w, need_ctx_out):
    def prep(t):
        q, k, v, g, lr_f, lr_b = split_cols(t, B_SPLITS)
        q = to_heads(q, GLA_HEADS).astype(jnp.float32) * (GLA_DK ** -0.5)
        k = to_heads(k, GLA_HEADS).astype(jnp.float32)
        v = to_heads(v, GLA_HEADS).astype(jnp.float32)
        return q, k, v, g, gla_log_decay(lr_f, w_gate_f, b_gate_f), gla_log_decay(lr_b, w_gate_b, b_gate_b)

    def finish(o, g):
        o = rms_norm(o.transpose(0, 2, 1, 3), norm_w)
        b, l = o.shape[0], o.shape[1]
        return o.reshape(b, l, GLA_V_W).astype(g.dtype) * jax.nn.silu(g)

    q_c, k_c, v_c, g_c, laf_c, lab_c = prep(b_ctx)
    s0 = jnp.zeros((q_c.shape[0], GLA_HEADS, GLA_DK, GLA_DV), jnp.float32)
    o_c, s_f, s_b = gla_bidir(q_c, k_c, v_c, laf_c, lab_c, s0, s0)
    q, k, v, g, laf, lab = prep(b_lat)
    o_l, _, _ = gla_bidir(q, k, v, laf, lab, s_f, s_b)
    y_ctx = finish(o_c, g_c) if need_ctx_out else None
    return finish(o_l, g), y_ctx

def na_mixer(c_lat, c_ctx, rpb, need_ctx_out):
    q, k, v = [to_heads(t, NA_HEADS) for t in split_cols(c_lat, C_SPLITS)]
    q_c, k_c, v_c = [to_heads(t, NA_HEADS) for t in split_cols(c_ctx, C_SPLITS)]
    b, h, l, d = q.shape
    rows = l // GRID_W
    kh = min(NA_KH, rows)
    grid = lambda t: t.reshape(b, h, rows, GRID_W, d)
    qg, kg, vg = grid(q * NA_SCALE), grid(k), grid(v)
    col = jnp.arange(GRID_W)
    col_start = jnp.clip(col - NA_KW // 2, 0, GRID_W - NA_KW)
    col_mask = (col[None, :] >= col_start[:, None]) & (col[None, :] < col_start[:, None] + NA_KW)
    col_off = jnp.clip(col[None, :] - col[:, None] + NA_KW - 1, 0, 2 * NA_KW - 2)
    band = kh * GRID_W

    def row_attend(r):
        r0 = jnp.clip(r - kh // 2, 0, rows - kh)
        kb = lax.dynamic_slice_in_dim(kg, r0, kh, axis=2)
        vb = lax.dynamic_slice_in_dim(vg, r0, kh, axis=2)
        qr = lax.dynamic_index_in_dim(qg, r, axis=2, keepdims=False)
        row_off = r0 + jnp.arange(kh) - r + NA_KH - 1
        bias = rpb[:, row_off[:, None, None], col_off[None, :, :]].transpose(0, 2, 1, 3)
        s_band = jnp.einsum('bhqd,bhrkd->bhqrk', qr, kb).astype(jnp.float32) + bias.astype(jnp.float32)
        s_band = jnp.where(col_mask[:, None, :], s_band, -jnp.inf)
        s_ctx = jnp.einsum('bhqd,bhkd->bhqk', qr, k_c).astype(jnp.float32)
        s = jnp.concatenate([s_band.reshape(b, h, GRID_W, band), s_ctx], axis=-1)
        p = jax.nn.softmax(s, axis=-1).astype(v.dtype)
        p_band = p[..., :band].reshape(b, h, GRID_W, kh, GRID_W)
        return (jnp.einsum('bhqrk,bhrkd->bhqd', p_band, vb)
                + jnp.einsum('bhqk,bhkd->bhqd', p[..., band:], v_c))

    o = lax.map(row_attend, jnp.arange(rows))
    y_lat = o.transpose(1, 0, 3, 2, 4).reshape(b, l, h * d)
    y_ctx = from_heads(dense_attend(q_c * NA_SCALE, k_c, v_c)) if need_ctx_out else None
    return y_lat, y_ctx

def merge_branches(ya, yb, yc, gates, w_a_o, w_b_o, w_c_o, w_out):
    ga, gb, gc = jnp.split(jax.nn.sigmoid(gates), N_BRANCH, axis=-1)
    return (ga * (ya @ w_a_o) + gb * (yb @ w_b_o) + gc * (yc @ w_c_o)) @ w_out

def swiglu(u, w_ffn_in, w_ffn_out):
    gate, up = jnp.split(u @ w_ffn_in, 2, axis=-1)
    return (jax.nn.silu(gate) * up) @ w_ffn_out

def hybrid_layer(h, hc, mod, modc, norm1_w, w_in, mla_q_norm_w, mla_kv_norm_w, mla_w_q_up, mla_w_kv_up,
                 gla_w_gate_f, gla_b_gate_f, gla_w_gate_b, gla_b_gate_b, gla_norm_w, na_rpb,
                 w_a_o, w_b_o, w_c_o, w_out, norm2_w, w_ffn_in, w_ffn_out, cos, sin, need_ctx_out):
    sh1, sc1, g1, sh2, sc2, g2 = mod
    csh1, csc1, cg1, csh2, csc2, cg2 = modc
    z = modulate(rms_norm(h, norm1_w), sh1, sc1) @ w_in
    zc = modulate(rms_norm(hc, norm1_w), csh1, csc1) @ w_in
    a, bb, cc, gates = split_cols(z, GROUP_SPLITS)
    a_c, bb_c, cc_c, gates_c = split_cols(zc, GROUP_SPLITS)
    ya, ya_c = mla_mixer(a, a_c, mla_q_norm_w, mla_kv_norm_w, mla_w_q_up, mla_w_kv_up, cos, sin, need_ctx_out)
    yb, yb_c = gla_mixer(bb, bb_c, gla_w_gate_f, gla_b_gate_f, gla_w_gate_b, gla_b_gate_b, gla_norm_w, need_ctx_out)
    yc, yc_c = na_mixer(cc, cc_c, na_rpb, need_ctx_out)
    h = h + g1 * merge_branches(ya, yb, yc, gates, w_a_o, w_b_o, w_c_o, w_out)
    h = h + g2 * swiglu(modulate(rms_norm(h, norm2_w), sh2, sc2), w_ffn_in, w_ffn_out)
    if need_ctx_out:
        hc = hc + cg1 * merge_branches(ya_c, yb_c, yc_c, gates_c, w_a_o, w_b_o, w_c_o, w_out)
        hc = hc + cg2 * swiglu(modulate(rms_norm(hc, norm2_w), csh2, csc2), w_ffn_in, w_ffn_out)
    return h, hc

def first_inputs(seed: int = 0) -> dict:
    key = jax.random.key(seed)
    ks = iter(jax.random.split(key, 32))

    def nrm(shape, scale):
        return jax.random.normal(next(ks), shape, jnp.float32) * scale

    L, D = DEPTH, D_MODEL
    return {
        "x": nrm((BATCH, SEQ, D), 1.0),
        "c": nrm((BATCH, D), 1.0),
        "ctx": nrm((BATCH, CTX_LEN, D), 1.0),
        "c_ctx": nrm((D,), 1.0),
        "w_mod": nrm((L, D, 6 * D), 0.5 * D ** -0.5),
        "b_mod": nrm((L, 6 * D), 0.02),
        "norm1_w": 1.0 + nrm((L, D), 0.02),
        "w_in": nrm((L, D, IN_WIDTH), D ** -0.5),
        "mla_q_norm_w": 1.0 + nrm((L, MLA_Q_RANK), 0.02),
        "mla_kv_norm_w": 1.0 + nrm((L, MLA_KV_RANK), 0.02),
        "mla_w_q_up": nrm((L, MLA_Q_RANK, MLA_HEADS * (MLA_NOPE + MLA_ROPE)), MLA_Q_RANK ** -0.5),
        "mla_w_kv_up": nrm((L, MLA_KV_RANK, MLA_HEADS * (MLA_NOPE + MLA_V)), MLA_KV_RANK ** -0.5),
        "gla_w_gate_f": nrm((L, GLA_GATE_RANK, GLA_QK_W), GLA_GATE_RANK ** -0.5),
        "gla_b_gate_f": nrm((L, GLA_QK_W), 0.1),
        "gla_w_gate_b": nrm((L, GLA_GATE_RANK, GLA_QK_W), GLA_GATE_RANK ** -0.5),
        "gla_b_gate_b": nrm((L, GLA_QK_W), 0.1),
        "gla_norm_w": 1.0 + nrm((L, GLA_DV), 0.02),
        "na_rpb": nrm((L, NA_HEADS, 2 * NA_KH - 1, 2 * NA_KW - 1), 0.1),
        "w_a_o": nrm((L, MLA_OUT_W, D), MLA_OUT_W ** -0.5),
        "w_b_o": nrm((L, GLA_V_W, D), GLA_V_W ** -0.5),
        "w_c_o": nrm((L, NA_W, D), NA_W ** -0.5),
        "w_out": nrm((L, D, D), D ** -0.5),
        "norm2_w": 1.0 + nrm((L, D), 0.02),
        "w_ffn_in": nrm((L, D, 2 * FFN_HIDDEN), D ** -0.5),
        "w_ffn_out": nrm((L, FFN_HIDDEN, D), FFN_HIDDEN ** -0.5),
        "final_norm_w": 1.0 + nrm((D,), 0.02),
    }

def first_block(x, c, ctx, c_ctx, w_mod, b_mod, norm1_w, w_in, mla_q_norm_w, mla_kv_norm_w, mla_w_q_up,
              mla_w_kv_up, gla_w_gate_f, gla_b_gate_f, gla_w_gate_b, gla_b_gate_b, gla_norm_w, na_rpb,
              w_a_o, w_b_o, w_c_o, w_out, norm2_w, w_ffn_in, w_ffn_out, final_norm_w):
    cos, sin = axial_rope_tables(x.shape[1])
    c_act = jax.nn.silu(c)[:, None, :]
    cc_act = jax.nn.silu(c_ctx)
    h, hc = x, ctx
    for i in range(DEPTH):
        mod = jnp.split(c_act @ w_mod[i] + b_mod[i], 6, axis=-1)
        modc = jnp.split(cc_act @ w_mod[i] + b_mod[i], 6, axis=-1)
        h, hc = hybrid_layer(h, hc, mod, modc, norm1_w[i], w_in[i], mla_q_norm_w[i], mla_kv_norm_w[i],
                             mla_w_q_up[i], mla_w_kv_up[i], gla_w_gate_f[i], gla_b_gate_f[i],
                             gla_w_gate_b[i], gla_b_gate_b[i], gla_norm_w[i], na_rpb[i],
                             w_a_o[i], w_b_o[i], w_c_o[i], w_out[i], norm2_w[i], w_ffn_in[i],
                             w_ffn_out[i], cos, sin, i < DEPTH - 1)
    return rms_norm(h, final_norm_w)


_first_inputs = first_inputs


def first_inputs(seed=0):
    import zlib

    import numpy as np

    out = dict(_first_inputs(seed))
    spreads = {}
    factors = {}
    for name, (base, spread) in spreads.items():
        noise = np.random.default_rng([zlib.crc32(name.encode()), seed]).standard_normal(out[name].shape)
        drawn = base * np.exp(spread * noise) if base else spread * noise
        out[name] = __import__('jax').numpy.asarray(drawn.astype(out[name].dtype))
    for name, factor in factors.items():
        out[name] = (out[name] * factor).astype(out[name].dtype)
    return out


_narrow_inputs = first_inputs


def first_inputs(seed=0):
    out = dict(_narrow_inputs(seed))
    wider = {'norm1_w': 9.83,
     'mla_q_norm_w': 12.0,
     'mla_kv_norm_w': 12.0,
     'mla_w_q_up': 3.02,
     'gla_w_gate_f': 3.23,
     'gla_b_gate_f': 12.0,
     'gla_w_gate_b': 3.6,
     'gla_b_gate_b': 12.0,
     'gla_norm_w': 12.0,
     'na_rpb': 12.0,
     'norm2_w': 7.37,
     'final_norm_w': 3.16}
    for name, times in wider.items():
        mean = out[name].mean()
        out[name] = (mean + times * (out[name] - mean)).astype(out[name].dtype)
    return out


HEAD_DIM = 64
MIX_WIDTH = D_MODEL
DIFF_WIDTH = MIX_WIDTH // 2
DIFF_HEADS = DIFF_WIDTH // (2 * HEAD_DIM)
SWA_WIDTH = MIX_WIDTH - DIFF_WIDTH
SWA_Q_HEADS = SWA_WIDTH // HEAD_DIM
SWA_KV_HEADS = 2
SWA_GROUP = SWA_Q_HEADS // SWA_KV_HEADS
WINDOW = 128
BLOCK = 128
D_FF = ((8 * D_MODEL // 3 + 127) // 128) * 128
ROPE_THETA = 10000.0
ALPHA = (2.0 * DEPTH) ** 0.25
BETA = (8.0 * DEPTH) ** -0.25
LN_EPS = 1e-5
RMS_EPS = 1e-5

DQ = DIFF_HEADS * 2 * HEAD_DIM
DK = DIFF_HEADS * 2 * HEAD_DIM
DV = DIFF_HEADS * 2 * HEAD_DIM
SQ = SWA_Q_HEADS * HEAD_DIM
SK = SWA_KV_HEADS * HEAD_DIM
SV = SWA_KV_HEADS * HEAD_DIM
IN_COLS = DQ + DK + DV + SQ + SK + SV


def layer_norm(x, g, b):
    xf = x.astype(jnp.float32)
    mu = jnp.mean(xf, axis=-1, keepdims=True)
    var = jnp.mean(jnp.square(xf - mu), axis=-1, keepdims=True)
    y = (xf - mu) * lax.rsqrt(var + LN_EPS) * g.astype(jnp.float32) + b.astype(jnp.float32)
    return y.astype(x.dtype)

def swiglu_2(x, w_in, w_out):
    h = x @ w_in
    gate, up = h[..., :D_FF], h[..., D_FF:]
    return (jax.nn.silu(gate) * up) @ w_out

def rope_tables(positions):
    inv = jnp.power(ROPE_THETA, -jnp.arange(0, HEAD_DIM, 2, dtype=jnp.float32) / HEAD_DIM)
    ang = positions.astype(jnp.float32)[..., None] * inv
    ang = jnp.concatenate([ang, ang], axis=-1)[:, :, None, :]
    return jnp.cos(ang), jnp.sin(ang)

def apply_rope_2(t, cos, sin):
    half = HEAD_DIM // 2
    t1, t2 = t[..., :half], t[..., half:]
    rot = jnp.concatenate([-t2, t1], axis=-1)
    return (t * cos.astype(t.dtype) + rot * sin.astype(t.dtype)).astype(t.dtype)

def diff_attention(q, k, v, lam, subln_g, lambda_init):
    B, S = q.shape[0], q.shape[1]
    nb = S // BLOCK
    scale = HEAD_DIM ** -0.5
    qb = q.reshape(B, nb, BLOCK, DIFF_HEADS, 2, HEAD_DIM).transpose(1, 0, 2, 3, 4, 5)

    def one_block(q_blk):
        s = jnp.einsum('bqhcd,bkhcd->bhcqk', q_blk, k).astype(jnp.float32) * scale
        p = jax.nn.softmax(s, axis=-1)
        a = p[:, :, 0] - lam * p[:, :, 1]
        return jnp.einsum('bhqk,bkhe->bqhe', a.astype(v.dtype), v)

    o = lax.map(one_block, qb)
    o = o.transpose(1, 0, 2, 3, 4).reshape(B, S, DIFF_HEADS, 2 * HEAD_DIM)
    of = o.astype(jnp.float32)
    of = of * lax.rsqrt(jnp.mean(jnp.square(of), axis=-1, keepdims=True) + RMS_EPS)
    of = of * subln_g.astype(jnp.float32) * (1.0 - lambda_init)
    return of.astype(v.dtype).reshape(B, S, DIFF_WIDTH)

def band_mask(S):
    nb = S // BLOCK
    qpos = jnp.arange(nb)[:, None, None] * BLOCK + jnp.arange(BLOCK)[None, :, None]
    kpos = (jnp.arange(nb)[:, None, None] - 1) * BLOCK + jnp.arange(3 * BLOCK)[None, None, :]
    return (jnp.abs(qpos - kpos) <= WINDOW) & (kpos >= 0) & (kpos < S)

def swa_sink_attention(q, k, v, sink, mask):
    B, S = q.shape[0], q.shape[1]
    nb = S // BLOCK
    scale = HEAD_DIM ** -0.5
    qb = q.reshape(B, nb, BLOCK, SWA_KV_HEADS, SWA_GROUP, HEAD_DIM)

    def band(t):
        tp = jnp.pad(t, ((0, 0), (BLOCK, BLOCK), (0, 0), (0, 0)))
        tp = tp.reshape(B, nb + 2, BLOCK, SWA_KV_HEADS, HEAD_DIM)
        return jnp.concatenate([tp[:, :-2], tp[:, 1:-1], tp[:, 2:]], axis=2)

    kb, vb = band(k), band(v)
    s = jnp.einsum('bnqhgd,bnkhd->bnhgqk', qb, kb).astype(jnp.float32) * scale
    s = jnp.where(mask[None, :, None, None, :, :], s, -jnp.inf)
    sk = sink.astype(jnp.float32).reshape(1, 1, SWA_KV_HEADS, SWA_GROUP, 1, 1)
    m = jnp.maximum(jnp.max(s, axis=-1, keepdims=True), sk)
    e = jnp.exp(s - m)
    p = e / (jnp.sum(e, axis=-1, keepdims=True) + jnp.exp(sk - m))
    o = jnp.einsum('bnhgqk,bnkhd->bnqhgd', p.astype(v.dtype), vb)
    return o.reshape(B, S, SWA_WIDTH)

def hybrid_mixer(x, cos, sin, mask, w_in, w_out, lam_vec, subln_g, sink, lambda_init):
    B, S = x.shape[0], x.shape[1]
    h = x @ w_in
    o0 = 0
    dq = h[..., o0:o0 + DQ]; o0 += DQ
    dk = h[..., o0:o0 + DK]; o0 += DK
    dv = h[..., o0:o0 + DV]; o0 += DV
    sq = h[..., o0:o0 + SQ]; o0 += SQ
    sk = h[..., o0:o0 + SK]; o0 += SK
    sv = h[..., o0:o0 + SV]

    dq = apply_rope_2(dq.reshape(B, S, 2 * DIFF_HEADS, HEAD_DIM), cos, sin)
    dk = apply_rope_2(dk.reshape(B, S, 2 * DIFF_HEADS, HEAD_DIM), cos, sin)
    dq = dq.reshape(B, S, DIFF_HEADS, 2, HEAD_DIM)
    dk = dk.reshape(B, S, DIFF_HEADS, 2, HEAD_DIM)
    dv = dv.reshape(B, S, DIFF_HEADS, 2 * HEAD_DIM)
    lv = lam_vec.astype(jnp.float32)
    lam = jnp.exp(jnp.sum(lv[0] * lv[1])) - jnp.exp(jnp.sum(lv[2] * lv[3])) + lambda_init
    y_diff = diff_attention(dq, dk, dv, lam, subln_g, lambda_init)

    sq = apply_rope_2(sq.reshape(B, S, SWA_Q_HEADS, HEAD_DIM), cos, sin)
    sk = apply_rope_2(sk.reshape(B, S, SWA_KV_HEADS, HEAD_DIM), cos, sin)
    sv = sv.reshape(B, S, SWA_KV_HEADS, HEAD_DIM)
    y_swa = swa_sink_attention(sq, sk, sv, sink, mask)

    return jnp.concatenate([y_diff, y_swa], axis=-1) @ w_out

def second_inputs(seed: int = 0) -> dict:
    key = jax.random.key(seed)
    ks = jax.random.split(key, 14)
    f32 = jnp.float32
    x = jax.random.normal(ks[0], (BATCH, SEQ, D_MODEL), f32)
    positions = jnp.broadcast_to(jnp.arange(SEQ, dtype=jnp.int32)[None, :], (BATCH, SEQ))
    col_scale = jnp.concatenate([
        jnp.ones((DQ + DK,), f32), jnp.full((DV,), BETA, f32),
        jnp.ones((SQ + SK,), f32), jnp.full((SV,), BETA, f32)])
    w_in = jax.random.normal(ks[1], (DEPTH, D_MODEL, IN_COLS), f32) * (D_MODEL ** -0.5) * col_scale
    w_out = jax.random.normal(ks[2], (DEPTH, MIX_WIDTH, D_MODEL), f32) * (MIX_WIDTH ** -0.5) * BETA
    diff_lambda = jax.random.normal(ks[3], (DEPTH, 4, HEAD_DIM), f32) * 0.1
    diff_subln_g = 1.0 + 0.02 * jax.random.normal(ks[4], (DEPTH, 2 * HEAD_DIM), f32)
    swa_sink = 0.5 * jax.random.normal(ks[5], (DEPTH, SWA_Q_HEADS), f32)
    ffn1_w_in = jax.random.normal(ks[6], (DEPTH, D_MODEL, 2 * D_FF), f32) * (D_MODEL ** -0.5)
    ffn1_w_out = jax.random.normal(ks[7], (DEPTH, D_FF, D_MODEL), f32) * (D_FF ** -0.5) * BETA
    ffn2_w_in = jax.random.normal(ks[8], (DEPTH, D_MODEL, 2 * D_FF), f32) * (D_MODEL ** -0.5)
    ffn2_w_out = jax.random.normal(ks[9], (DEPTH, D_FF, D_MODEL), f32) * (D_FF ** -0.5) * BETA
    ln_g = 1.0 + 0.02 * jax.random.normal(ks[10], (DEPTH, 3, D_MODEL), f32)
    ln_b = 0.02 * jax.random.normal(ks[11], (DEPTH, 3, D_MODEL), f32)
    return {"x": x, "positions": positions, "w_in": w_in, "w_out": w_out,
            "diff_lambda": diff_lambda, "diff_subln_g": diff_subln_g, "swa_sink": swa_sink,
            "ffn1_w_in": ffn1_w_in, "ffn1_w_out": ffn1_w_out,
            "ffn2_w_in": ffn2_w_in, "ffn2_w_out": ffn2_w_out,
            "ln_g": ln_g, "ln_b": ln_b}

def second_block(x, positions, w_in, w_out, diff_lambda, diff_subln_g, swa_sink,
              ffn1_w_in, ffn1_w_out, ffn2_w_in, ffn2_w_out, ln_g, ln_b):
    S = x.shape[1]
    cos, sin = rope_tables(positions)
    mask = band_mask(S)
    for l in range(DEPTH):
        lambda_init = 0.8 - 0.6 * math.exp(-0.3 * l)
        x = layer_norm(ALPHA * x + 0.5 * swiglu_2(x, ffn1_w_in[l], ffn1_w_out[l]), ln_g[l, 0], ln_b[l, 0])
        mix = hybrid_mixer(x, cos, sin, mask, w_in[l], w_out[l], diff_lambda[l],
                           diff_subln_g[l], swa_sink[l], lambda_init)
        x = layer_norm(ALPHA * x + mix, ln_g[l, 1], ln_b[l, 1])
        x = layer_norm(ALPHA * x + 0.5 * swiglu_2(x, ffn2_w_in[l], ffn2_w_out[l]), ln_g[l, 2], ln_b[l, 2])
    return x


def setup_inputs(seed=0):
    out = dict(first_inputs(seed))
    for name, value in second_inputs(seed + 1).items():
        if name != "x":
            out[name + "_2"] = value
    return out


def reference(
    x, c, ctx, c_ctx, w_mod, b_mod, norm1_w, w_in, mla_q_norm_w, mla_kv_norm_w, mla_w_q_up,
    mla_w_kv_up, gla_w_gate_f, gla_b_gate_f, gla_w_gate_b, gla_b_gate_b, gla_norm_w, na_rpb,
    w_a_o, w_b_o, w_c_o, w_out, norm2_w, w_ffn_in, w_ffn_out, final_norm_w, positions_2, w_in_2,
    w_out_2, diff_lambda_2, diff_subln_g_2, swa_sink_2, ffn1_w_in_2, ffn1_w_out_2, ffn2_w_in_2,
    ffn2_w_out_2, ln_g_2, ln_b_2,
):
    x = first_block(
        x, c, ctx, c_ctx, w_mod, b_mod, norm1_w, w_in, mla_q_norm_w, mla_kv_norm_w, mla_w_q_up,
        mla_w_kv_up, gla_w_gate_f, gla_b_gate_f, gla_w_gate_b, gla_b_gate_b, gla_norm_w, na_rpb,
        w_a_o, w_b_o, w_c_o, w_out, norm2_w, w_ffn_in, w_ffn_out, final_norm_w,
    )
    return second_block(
        x, positions_2, w_in_2, w_out_2, diff_lambda_2, diff_subln_g_2, swa_sink_2, ffn1_w_in_2,
        ffn1_w_out_2, ffn2_w_in_2, ffn2_w_out_2, ln_g_2, ln_b_2,
    )


_drawn_inputs = setup_inputs


def setup_inputs(seed=0):
    import zlib

    import numpy as np

    out = dict(_drawn_inputs(seed))
    spreads = {}
    factors = {'diff_subln_g_2': 8.0, 'swa_sink_2': 8.0}
    for name, (base, spread) in spreads.items():
        noise = np.random.default_rng([zlib.crc32(name.encode()), seed]).standard_normal(out[name].shape)
        drawn = base * np.exp(spread * noise) if base else spread * noise
        out[name] = __import__('jax').numpy.asarray(drawn.astype(out[name].dtype))
    for name, factor in factors.items():
        out[name] = (out[name] * factor).astype(out[name].dtype)
    return out
```

```python
import math
from contextlib import ExitStack, contextmanager

import numpy as np

import concourse.bass as bass
from concourse import mybir

F32, F32R, BF16, I32 = mybir.dt.float32, mybir.dt.float32r, mybir.dt.bfloat16, mybir.dt.int32
ALU, ACT, AX = mybir.AluOpType, mybir.ActivationFunctionType, mybir.AxisListType

P = 128
D, KD = 1024, 8
S, T = 256, 512
L = 2
QR, KVR, NOPE, ROPE, HD = 384, 256, 64, 32, 64
QH = NOPE + ROPE
HEADS = 8
F, FT = 2816, 22
GRID_W, NA_KH, NA_KW = 64, 8, 16
EPS1, EPS2 = 1e-6, 1e-5
ALPHA = (2.0 * L) ** 0.25
MLA_SCALE = QH ** -0.5
NEG = -1e30
C_KV, C_KR = QR, QR + KVR
C_GQ = C_KR + ROPE
C_GK, C_GV, C_GG = C_GQ + 256, C_GQ + 512, C_GQ + 1024
C_LR = C_GG + 512
C_NQ = C_LR + 32
C_NK, C_NV, C_GATE = C_NQ + 512, C_NQ + 1024, C_NQ + 1536
PAR = {}
for _name, _n in (("c", 8), ("c_ctx", 8), ("b_mod", 96), ("norm1_w", 16), ("norm2_w", 16),
                  ("mla_q_norm_w", 6), ("mla_kv_norm_w", 4), ("final_norm_w", 8), ("ln_g_2", 48), ("ln_b_2", 48)):
    PAR[_name] = (sum(n for _, n in PAR.values()), _n)
PAR_TILES = (("c", "c_ctx", "b_mod", "norm1_w"), ("norm2_w", "mla_q_norm_w", "mla_kv_norm_w", "final_norm_w", "ln_g_2"),
             ("ln_b_2",))
CONST = {}
for _name, _n in (("ident", 128), ("rot1", 96), ("tri_f", 128), ("tri_b", 128), ("strict_f", 128),
                  ("strict_b", 128), ("cos1", 256), ("sin1", 256), ("rot2", 128), ("swap", 128), ("band", 512), ("inv", 1)):
    CONST[_name] = (sum(n for _, n in CONST.values()), _n)
N_CONST1 = CONST["rot2"][0]
N_CONST = sum(n for _, n in CONST.values())


def constants():
    c = np.zeros((P, N_CONST), np.float32)

    def put(name, a):
        c[:a.shape[0], CONST[name][0]:CONST[name][0] + a.shape[1]] = a

    put("ident", np.eye(P, dtype=np.float32))
    i, j = np.arange(P)[:, None], np.arange(P)[None, :]
    r1 = np.zeros((QH, QH), np.float32)
    for t in range(ROPE // 2):
        r1[NOPE + ROPE // 2 + t, NOPE + t] = -1.0
        r1[NOPE + t, NOPE + ROPE // 2 + t] = 1.0
    put("rot1", r1)
    same = (i // 64) == (j // 64)
    put("tri_f", (same & (i <= j)) / np.float32(16))
    put("tri_b", (same & (i >= j)) / np.float32(16))
    put("strict_f", (same & (i > j)) / np.float32(16))
    put("strict_b", (same & (i < j)) / np.float32(16))
    t = np.arange(S)
    n_freq = ROPE // 4
    freq = (np.float32(10000.0) ** (-np.arange(n_freq, dtype=np.float32) / n_freq)).astype(np.float32)
    ang = np.concatenate([(t // GRID_W).astype(np.float32)[:, None] * freq,
                          (t % GRID_W).astype(np.float32)[:, None] * freq], -1)
    for name, fn in (("cos1", np.cos), ("sin1", np.sin)):
        a = np.zeros((QH, S), np.float32)
        a[NOPE:] = np.concatenate([fn(ang), fn(ang)], -1).T
        put(name, a)
    r2 = np.zeros((P, P), np.float32)
    for t in range(P):
        if t % 64 < 32:
            r2[t + 32, t] = -1.0
        else:
            r2[t - 32, t] = 1.0
    put("rot2", r2)
    put("swap", ((i + 64) % P == j).astype(np.float32))
    band = np.zeros((P, 2, S), np.float32)
    q, k = np.arange(P)[:, None], np.arange(S)[None, :]
    for n in range(2):
        band[:, n] = np.where(np.abs(q + P * n - k) <= 128, 0.0, NEG)
    put("band", band.reshape(P, 512))
    inv = np.power(np.float32(10000.0), -np.arange(0, 64, 2, dtype=np.float32) / np.float32(64)).astype(np.float32)
    put("inv", inv[np.arange(P) % 32][:, None])
    return c


class Signal:

    def __init__(self, sem, known):
        self.sem, self.known, self.marks, self.count = sem, known, {}, 0

    def tick(self, label=None, by=1):
        self.count += by
        if label is not None:
            self.marks[label] = (self.count, 0, 1)
        return self.sem, by

    def mark(self, label):
        self.marks[label] = (self.count, 0, 1)

    def at(self, label, turn=None):
        if self.known is None:
            return self.sem, 1
        base, per, n = self.known[label]
        if turn is None:
            return self.sem, base + per * (n - 1)
        return self.sem, turn * per + base if per else base


def program(nc, a, out, known):
    signals = {}
    with ExitStack() as stack:
        def sem(name):
            return stack.enter_context(nc.semaphore(name))

        def signal(name):
            signals[name] = Signal(sem(name), known and known[name])
            return signals[name]

        @contextmanager
        def repeat(eng, turns):
            before = {n: (s.count, set(s.marks)) for n, s in signals.items()}
            with eng.Fori(0, turns) as it:
                yield it
            for n, s in signals.items():
                start, old = before[n]
                step = s.count - start
                if step:
                    for label in set(s.marks) - old:
                        s.marks[label] = (s.marks[label][0], step, turns)
                    s.count = start + step * turns

        pe_done, act_done = signal("pe_done"), signal("act_done")
        dve_done, pool_done = signal("dve_done"), signal("pool_done")
        loaded = signal("loaded")
        loaded2 = signal("loaded2")
        bias_loaded = signal("bias_loaded")
        bands_written = signal("bands_written")
        stored = signal("stored")
        landed = [sem(f"landed{i}") for i in range(3)]
        hi_ready, lo_ready, lo_ready_pool = sem("hi_ready"), sem("lo_ready"), sem("lo_ready_pool")
        panel_used = sem("panel_used")
        mod_taken = sem("mod_taken")
        silu_done, hid_done = sem("silu_done"), sem("hid_done")
        hid_hi, hid_lo = sem("hid_hi"), sem("hid_lo")
        gate_ready, merged = sem("gate_ready"), sem("merged")

        place = [((nc.sbuf_base + 63) // 64) * 64]

        def at(offset, name, shape, dt=F32):
            n = int(np.prod(shape[1:])) * (2 if dt == BF16 else 4)
            t = nc.alloc_sbuf_tensor_at(name, shape, dt, offset=offset)
            return t, offset + ((n + 31) // 32) * 32

        def sb(name, shape, dt=F32):
            t, place[0] = at(place[0], name, shape, dt)
            return t

        raw = [sb(f"raw{i}", [P, 2048]) for i in range(3)]
        whi = [sb(f"whi{i}", [P, 2048], F32R) for i in range(3)]
        wlo = [sb(f"wlo{i}", [P, 2048], F32R) for i in range(3)]
        h = sb("h", [P, KD, T])
        xh, xl = sb("xh", [P, KD, T], F32R), sb("xl", [P, KD, T], F32R)
        par = sb("par", [P, 2 * P + 48])
        mod = sb("mod", [P, 2 * L, 48])
        ch, cl = sb("ch", [P, 8, 2], F32R), sb("cl", [P, 8, 2], F32R)
        mul = sb("mul", [P, 2, 8])
        ones = sb("ones", [P, P])
        eps = sb("eps", [P, 3])
        zero = sb("zero", [P, 512], BF16)
        bands = nc.dram_tensor("bias_bands", (L, 7, HEADS, GRID_W, GRID_W), F32, kind="Internal").ap()
        cst = sb("cst", [P, N_CONST1])
        gln = sb("gln", [P, L, P])
        wg = sb("wg", [P, 512])
        stat = sb("stat", [P, T])
        sq = sb("sq", [P, 2, T])
        y = sb("y", [P, 12, T])
        scratch = place[0]
        y_at = scratch - 12 * T * 4
        modt, _ = at(y_at, "modt", [P, 48 * P])
        gates, _ = at(y_at - 3 * T * 4, "gates", [P, 3, T])

        def const(name, rows=P):
            o, n = CONST[name]
            return cst[0:rows, o:o + n]

        def col(name, k):
            return par[:, PAR[name][0] + k:PAR[name][0] + k + 1]

        psum = stack.enter_context(nc.psum_tensor("psum", [P, 8, 512], F32))
        bank = [psum[:, b, :] for b in range(8)]
        ident = const("ident")

        o = scratch
        xtok, o = at(o, "xtok", [P, 4, D])
        ptok, o = at(o, "ptok", [P, 3, P])
        o = scratch
        vtok, o = at(o, "vtok", [P, 4, 512])
        qdh, o = at(o, "qdh", [P, 3, T], F32R)
        qdl, o = at(o, "qdl", [P, 3, T], F32R)
        kvh, o = at(o, "kvh", [P, 2, T], F32R)
        kvl, o = at(o, "kvl", [P, 2, T], F32R)
        kr, o = at(o, "kr", [P, T])
        o_att = o
        qt, o = at(o, "qt", [P, 2, T])
        kt, o = at(o, "kt", [P, 2, T])
        pr, o = at(o, "pr", [P, 2, T])
        prt, o = at(o, "prt", [P, 2, T])
        ytok, _ = at(y_at + 4 * T * 4, "ytok", [P, 4, 512])
        downs, _ = at(o_att, "downs", [P, 5, T])
        rt, _ = at(y_at + 8 * T * 4, "rt", [P, S])
        stat2, _ = at(y_at + 10 * T * 4, "stat2", [P, T])
        st8, _ = at(y_at + 9 * T * 4, "st8", [P, 16])
        top = o
        o = scratch
        gq, o = at(o, "gq", [P, 2, T])
        gk, o = at(o, "gk", [P, 2, T])
        gv, o = at(o, "gv", [P, 4, 512])
        la, o = at(o, "la", [P, 4, 512])
        ktok, _ = at(y_at + 8 * T * 4, "ktok", [P, 4, S])
        qdec, o = at(o, "qdec", [P, 2, T])
        kinv, o = at(o, "kinv", [P, 2, T])
        kend, o = at(o, "kend", [P, 4, S])
        expc, _ = at(y_at + 10 * T * 4, "expc", [P, 2, T])
        o_t = o
        lr, _ = at(o_t, "lr", [P, T])
        o = o_t + 2048
        ez, _ = at(y_at + 4 * T * 4, "ez", [P, 4, 512])
        attm, _ = at(y_at + 4 * T * 4, "attm", [P, 2, 512])
        state, _ = at(y_at - 2 * T * 4, "state", [P, 2, 2, S])
        gst, o = at(o, "gst", [P, 16])
        top = max(top, o)
        o = scratch
        nv, o = at(o, "nv", [P, 4, 512])
        nq, o = at(o, "nq", [P, 4, T])
        nk, o = at(o, "nk", [P, 4, T])
        nbias, o = at(o, "nbias", [P, HEADS, 6, 64])
        npr, o = at(o, "npr", [P, 2, T])
        nprt, o = at(o, "nprt", [P, 2, T])
        nst, o = at(o, "nst", [P, 16])
        nytok, o = at(o, "nytok", [P, 1, 512])
        top = max(top, o)
        o = scratch
        yh, o = at(o, "yh", [P, 12, T], F32R)
        mt, o = at(o, "mt", [P, 3, T])
        mf, o = at(o, "mf", [P, KD, T])
        top = max(top, o)
        yl, _ = at(y_at, "yl", [P, 12, T], F32R)
        h_n, _ = at(scratch, "h_n", [P, 3, T])
        o = scratch
        hidf, o = at(o, "hidf", [P, 2, S])
        sg, o = at(o, "sg", [P, 2, S])
        hidh, o = at(o, "hidh", [P, 2, 2, S], F32R)
        hidl, o = at(o, "hidl", [P, 2, 2, S], F32R)
        cst2, o = at(o, "cst2", [P, N_CONST - N_CONST1])
        cos2, o = at(o, "cos2", [P, S])
        sin2, o = at(o, "sin2", [P, S])
        subln, o = at(o, "subln", [P, L, P])
        sink, o = at(o, "sink", [P, L, 8])
        lamv, o = at(o, "lamv", [P, L, 4, 64])
        lam, o = at(o, "lam", [P, 2 * L])
        pos, o = at(o, "pos", [P, S], I32)
        ang, o = at(o, "ang", [P, 3, S])
        dvt, o = at(o, "dvt", [P, 2, 640])
        rtmp, o = at(o, "rtmp", [P, 2, S])
        ap_, o = at(o, "ap_", [P, 2, T])
        apt, o = at(o, "apt", [P, 2, S])
        ast, o = at(o, "ast", [P, 24])
        ytok2, _ = at(y_at + 14 * S * 4, "ytok2", [P, 2, D])
        ed, o = at(o, "ed", [P, 2, T])
        top = max(top, o)
        f2, _ = at(y_at, "f2", [P, 14, S])
        assert top <= nc.sbuf_usable_end, (top, nc.sbuf_usable_end)

        def prd(j):
            return ed[:, j % 2, :]

        def score_banks(n):
            return bank[n % 3], bank[(6, 7, 3)[n % 3]]

        def turned_at(tag, j, nk):
            return bank[4][:, S * (j % 2):S * (j % 2) + nk] if tag[0] == "att2" else bank[3 + j % 2][:, 0:nk]

        def out_at(dv):
            return bank[5][:, 0:dv]

        def ln_bank(tag):
            return 2 if tag[0] == "out2" else 6

        def ln_col(tag):
            name, l_ = tag
            return 24 * l_ + 8 * ("ffn1", "out2", "ffn2").index(name)

        def const2(name):
            o_, n = CONST[name]
            return cst2[:, o_ - N_CONST1:o_ - N_CONST1 + n]

        def rows(w, k0, nk):
            return w[k0 * P:(k0 + nk) * P, :].rearrange("(k p) n -> p k n", p=P)

        def full(w, nk, c0, n):
            k = nk // 2
            return nk * n, lambda it: [((0, k, n), rows(w, 0, k)[:, :, c0:c0 + n]),
                                       ((k * n, nk - k, n), rows(w, k, nk - k)[:, :, c0:c0 + n])]

        def dyn(w, k0, nk, base, step, n):
            return lambda it: rows(w, k0, nk)[:, :, bass.ds(it * step + base, n)]

        def mod_panel(l, j, first):
            c0 = 256 * j + 768 * first
            s0, s1 = dyn(a["w_mod"][l], 0, 4, c0, 768, 256), dyn(a["w_mod"][l], 4, 4, c0, 768, 256)
            return 2048, lambda it: [((0, 4, 256), s0(it)), ((1024, 4, 256), s1(it))]

        def merge_panels(l):
            g = [dyn(a["w_in"][l], 0, 8, C_GATE + D * b, P, P) for b in range(3)]
            yo = [dyn(a[w][l], 0, 4, 0, P, P) for w in ("w_a_o", "w_b_o", "w_c_o")]
            return [(2048, lambda it: [((0, 8, P), g[0](it)), ((1024, 8, P), g[1](it))]),
                    (2048, lambda it: [((0, 8, P), g[2](it)), ((1024, 4, P), yo[0](it)), ((1536, 4, P), yo[1](it))]),
                    (512, lambda it: [((0, 4, P), yo[2](it))])]

        def ffn_in_panel(w, tile, step):
            g, u = dyn(w, 0, 8, P * tile, P * step, P), dyn(w, 0, 8, F + P * tile, P * step, P)
            return 2048, lambda it: [((0, 8, P), g(it)), ((1024, 8, P), u(it))]

        def ffn_out_panel(w, pair, step):
            def parts(it):
                r0 = it * (2 * P * step) + 2 * P * pair
                return [((1024 * j, 1, D), w[bass.ds(r0 + P * j, P), :].unsqueeze(1)) for j in range(2)]
            return 2048, parts

        segments, sizes = [], []

        def line(*panels):
            first = len(sizes)
            segments.append((1, first, list(panels)))
            sizes.extend(s for s, _ in panels)
            return first

        def loop(turns, *panels):
            first = len(sizes)
            segments.append((turns, first, list(panels)))
            sizes.extend(s for _ in range(turns) for s, _ in panels)
            return first

        def ffn_panels(w_in, w_out, last=False):
            first = line(ffn_in_panel(w_in, 0, 0), ffn_in_panel(w_in, 1, 0))
            n = 4 if last else 5

            def body(t, step):
                return [ffn_in_panel(w_in, 2 + 4 * t, step), ffn_in_panel(w_in, 3 + 4 * t, step),
                        ffn_out_panel(w_out, 2 * t, step // 2),
                        ffn_in_panel(w_in, 4 + 4 * t, step), ffn_in_panel(w_in, 5 + 4 * t, step),
                        ffn_out_panel(w_out, 2 * t + 1, step // 2)]
            loop(n, *body(0, 4))
            if last:
                line(*body(4, 0))
            line(ffn_out_panel(w_out, 10, 0))
            return first

        base = {}
        for l in range(L):
            w = a["w_in"][l]
            base["mod", l] = line(*[mod_panel(l, j, 0) for j in range(3)])
            loop(7, *[mod_panel(l, j, 1) for j in range(3)])
            base["mla", l] = line(full(w, 8, 0, 256), full(w, 8, C_KV, 256), full(w, 8, 256, P),
                                  full(w, 8, C_KR - 64, QH), full(a["mla_w_q_up"][l], 3, 0, 384),
                                  full(a["mla_w_q_up"][l], 3, 384, 384), full(a["mla_w_kv_up"][l], 2, 0, D))
            base["gla", l] = line(full(w, 8, C_GQ, 256), full(w, 8, C_GK, 256), full(w, 8, C_GV, 256),
                                  full(w, 8, C_GV + 256, 256), full(w, 8, C_LR, 32), full(w, 8, C_GG, 256),
                                  full(w, 8, C_GG + 256, 256))
            base["na", l] = line(*[full(w, 8, C_NQ + 256 * j, 256) for j in range(6)])
            base["merge", l] = loop(8, *merge_panels(l))
            base["out", l] = line(*[full(a["w_out"][l], 8, 256 * j, 256) for j in range(4)])
            for part in range(2 if l == 0 else 1):
                base["ffn", l, part] = ffn_panels(a["w_ffn_in"][l], a["w_ffn_out"][l])
        for l in range(L):
            base["ffn1", l] = ffn_panels(a["ffn1_w_in_2"][l], a["ffn1_w_out_2"][l])
            base["win2", l] = line(*[full(a["w_in_2"][l], 8, 256 * j, 256) for j in range(9)])
            base["out2", l] = line(*[full(a["w_out_2"][l], 8, 256 * j, 256) for j in range(4)])
            base["ffn2", l] = ffn_panels(a["ffn2_w_in_2"][l], a["ffn2_w_out_2"][l], last=l == L - 1)
        N_PANELS = len(sizes)

        def load_panel(sp, parts, p0, per, it):
            slot = p0 % 3
            if p0 >= 3:
                sp.wait_ge(lo_ready, it * per + (p0 - 2))
                sp.wait_ge(lo_ready_pool, it * per + (p0 - 2))
            parts = parts(it)
            for n, ((c0, nk, width), src) in enumerate(parts):
                dst = raw[slot][:, c0:c0 + nk * width].rearrange("p (k n) -> p k n", k=nk)
                last = n == len(parts) - 1
                sp.dma_start(dst, src).then_inc(landed[slot], 16 * (3 - n) if last else 16)

        def in_range(p0, per, turns):
            assert all(sizes[p0] == sizes[p0 + per * t] for t in range(turns))

        def dve_cols(size):
            return (size * 5 // 8 + 31) // 32 * 32

        def split_act(act, p0, per=0, it=0, turns=1):
            if p0 >= N_PANELS:
                return
            in_range(p0, per, turns)
            slot, size = p0 % 3, sizes[p0]
            act.wait_ge(landed[slot], it * (per // 3 * 48) + 48 * (p0 // 3 + 1))
            if p0 >= 3:
                act.wait_ge(panel_used, it * per + (p0 - 2))
            act.activation(whi[slot][:, 0:size], raw[slot][:, 0:size], ACT.Copy).then_inc(hi_ready, 1)

        def split_lo(eng, sem_, cols, p0, per, it, turns):
            if p0 >= N_PANELS:
                return
            in_range(p0, per, turns)
            slot = p0 % 3
            eng.wait_ge(hi_ready, it * per + (p0 + 1))
            c0, c1 = cols(sizes[p0])
            eng.tensor_tensor(wlo[slot][:, c0:c1], raw[slot][:, c0:c1], whi[slot][:, c0:c1].bitcast(F32),
                              ALU.subtract).then_inc(sem_, 1)

        def split_dve(dve, p0, per=0, it=0, turns=1):
            split_lo(dve, lo_ready, lambda n: (0, dve_cols(n)), p0, per, it, turns)

        def split_pool(pool, p0, per=0, it=0, turns=1):
            split_lo(pool, lo_ready_pool, lambda n: (dve_cols(n), n), p0, per, it, turns)

        def open_panel(pe, p0, per=0, it=0):
            for s_ in (hi_ready, lo_ready, lo_ready_pool):
                pe.wait_ge(s_, it * per + (p0 + 1))
            return whi[p0 % 3], wlo[p0 % 3]

        def three(pe, dst, pairs, start=True, fresh=None):
            last = None
            for n, (sh, sl, mh, ml) in enumerate(pairs):
                if fresh is not None:
                    pe.wait_ge(*dve_done.at((fresh, "lo", n)))
                pe.matmul(dst, sh, mh, start=start and n == 0, stop=False, skip_group_check=True)
                pe.matmul(dst, sh, ml, start=False, stop=False, skip_group_check=True)
                last = pe.matmul(dst, sl, mh, start=False, stop=n == len(pairs) - 1, skip_group_check=True)
            return last

        ENG = {"pe": pe_done, "act": act_done, "dve": dve_done, "pool": pool_done}

        def stage(eng, me, name, prev):
            for other, s_ in ENG.items():
                if prev is not None:
                    eng.wait_ge(*s_.at(("end", prev)))

        def end(me, name):
            ENG[me].mark(("end", name))

        def squares_at(k, cols):
            if cols.stop - cols.start == S:
                return sq[:, k // 2 % 2, S * (k % 2):S * (k % 2) + S], 4
            return sq[:, k % 2, cols], 2

        def pe_sum(pe, tag, nk, bk, cols):
            for k in range(nk):
                pe.wait_ge(*act_done.at((tag, "sq", k)))
                pe.matmul(bank[bk][:, cols], ones[:], squares_at(k, cols)[0], start=k == 0, stop=k == nk - 1
                          ).then_inc(*pe_done.tick((tag, "sum", k)))

        def act_squares(act, tag, srcs, cols, eps_i, n_feat, bk, ready):
            for k, s_ in enumerate(srcs):
                ready(k)
                dst, lag = squares_at(k, cols)
                if k >= lag:
                    act.wait_ge(*pe_done.at((tag, "sum", k - lag)))
                act.activation(dst, s_, ACT.Square).then_inc(*act_done.tick((tag, "sq", k)))
            act.wait_ge(*pe_done.at((tag, "sum", len(srcs) - 1)))
            act.activation(stat[:, cols], bank[bk][:, cols], ACT.Sqrt, bias=eps[:, eps_i:eps_i + 1],
                           scale=1.0 / n_feat).then_inc(*act_done.tick((tag, "std")))

        def dve_rstd(dve, tag, cols, of=stat):
            dve.wait_ge(*act_done.at((tag, "std")))
            dve.reciprocal(of[:, cols], of[:, cols]).then_inc(*dve_done.tick((tag, "rstd")))
            dve.wait_ge(*dve_done.at((tag, "rstd")))

        KINDS = ((0, slice(0, S)), (1, slice(S, T)))

        block = stack.enter_context(nc.Block())

        def mix_tokens(l):
            return T if l < L - 1 else S

        def mla_items(l):
            lat = [(hd, q, 0, T) for hd in range(HEADS) for q in range(2)]
            ctx = [(hd, q, S, S) for hd in range(HEADS) for q in (2, 3)] if l < L - 1 else []
            return sorted(lat + ctx)

        @block.tensor
        def _(pe):
            def proj_f(p, cols, width, n0, n, nk, rhs_h, rhs_l, dst, fresh=None):
                hi, lo = whi[p % 3], wlo[p % 3]
                v = [t[:, 0:nk * width].rearrange("p (k n) -> p k n", k=nk)[:, :, n0:n0 + n] for t in (hi, lo)]
                return three(pe, dst, [(v[0][:, k, :], v[1][:, k, :], rhs_h[:, k, cols], rhs_l[:, k, cols])
                                       for k in range(nk)], fresh=fresh)

            def proj_t(p, tok, nk, lhs_h, lhs_l, dst, view):
                vh, vl = view(whi[p % 3]), view(wlo[p % 3])
                last = None
                for k in range(nk):
                    c = slice(P * tok, P * tok + P)
                    pe.matmul(dst, lhs_h[:, k, c], vh(k), start=k == 0, stop=False, skip_group_check=True)
                    pe.matmul(dst, lhs_h[:, k, c], vl(k), start=False, stop=False, skip_group_check=True)
                    last = pe.matmul(dst, lhs_l[:, k, c], vh(k), start=False, stop=k == nk - 1, skip_group_check=True)
                return last

            pe.wait_ge(*pool_done.at("setup"))
            pe.wait_ge(*loaded.at("inputs"))
            for t in range(4):
                for half in range(2):
                    g = 2 * t + half
                    for k in range(4):
                        m = pe.transpose(bank[g][:, k * P:(k + 1) * P], xtok[:, t, (4 * half + k) * P:(4 * half + k + 1) * P], ident)
                    m.then_inc(*pe_done.tick(("xT", g)))
            pe.wait_ge(*dve_done.at(("xT", 0)))
            for j, n in enumerate((P, 82, 48)):
                m = pe.transpose(bank[0][:, j * P:j * P + n], ptok[0:n, j, :], ident[0:n, 0:n])
            m.then_inc(*pe_done.tick("par"))
            end("pe", "load")

            def generic_f(l_tag, p, tiles, nk, width, cols, rhs_h, rhs_l, g0, banks=(4, 5, 6, 7), fresh=None):
                open_panel(pe, p)
                for i, (n0, n) in enumerate(tiles):
                    g = g0 + i
                    if g >= len(banks):
                        pe.wait_ge(*dve_done.at((l_tag, "ev", g - len(banks))))
                    m = proj_f(p, cols, width, n0, n, nk, rhs_h, rhs_l, bank[banks[g % len(banks)]][0:n, cols],
                               fresh=fresh if i == 0 else None)
                    if i == len(tiles) - 1:
                        m.then_inc(panel_used, 1)
                    else:
                        m.then_inc(*pe_done.tick((l_tag, "mm", g)))
                return g0 + len(tiles)

            def generic_t(l_tag, p, toks, g0, banks=(4, 5, 6, 7)):
                open_panel(pe, p)
                for i, t in enumerate(toks):
                    g = g0 + i
                    if g >= len(banks):
                        pe.wait_ge(*dve_done.at((l_tag, "ev", g - len(banks))))
                    m = proj_t(p, t, 8, xh, xl, bank[banks[g % len(banks)]][:, 0:256],
                               lambda w_: (lambda k: w_[:, 256 * k:256 * k + 256]))
                    if i == len(toks) - 1:
                        m.then_inc(panel_used, 1)
                    else:
                        m.then_inc(*pe_done.tick((l_tag, "mm", g)))
                return g0 + len(toks)

            def attend(tag, items, prep):
                N = len(items)
                for n in range(N + 3):
                    if n < N:
                        prep(n)
                        it_ = items[n]
                        if n >= 3:
                            pe.wait_ge(*act_done.at((tag, "exp", n - 3)))
                        m = it_["scores"](*score_banks(n)) if it_.get("diff") else it_["scores"](score_banks(n)[0])
                        m.then_inc(*pe_done.tick((tag, "s", n)))
                    if 2 <= n <= N + 1:
                        j = n - 2
                        pe.wait_ge(*(act_done if not items[j].get("diff") else dve_done).at((tag, "exp", j)))
                        lag = 1 if tag[0] == "att2" else 2
                        if j >= lag:
                            pe.wait_ge(*act_done.at((tag, "pt", j - lag)))
                        for c in range(items[j]["nk"] // P):
                            m = pe.transpose(turned_at(tag, j, items[j]["nk"])[:, c * P:(c + 1) * P],
                                             items[j]["p"](j)[:, c * P:(c + 1) * P], ident)
                        m.then_inc(*pe_done.tick((tag, "t", j)))
                    if n >= 3:
                        j = n - 3
                        pe.wait_ge(*act_done.at((tag, "pt", j)))
                        if j >= 1:
                            pe.wait_ge(*dve_done.at((tag, "y", j - 1)))
                        nkt = items[j]["nk"] // P
                        for c in range(nkt):
                            m = pe.matmul(out_at(items[j]["dv"]), items[j]["pt"](j)[:, c * P:(c + 1) * P],
                                          items[j]["v"][c], start=c == 0, stop=c == nkt - 1)
                        m.then_inc(*pe_done.tick((tag, "o", j)))

            def turn_y(tag, toks, src, n_tiles=4, engine=None):
                for i, t in enumerate(toks):
                    for b in range(n_tiles // 4):
                        g = i * (n_tiles // 4) + b
                        pe.wait_ge(*dve_done.at((tag, "ready", i)))
                        if g >= 2:
                            pe.wait_ge(*dve_done.at((tag, "turned", g - 2)))
                        for c in range(4):
                            m = pe.transpose(bank[6 + g % 2][:, c * P:(c + 1) * P], src(i)[:, (4 * b + c) * P:(4 * b + c + 1) * P], ident)
                        m.then_inc(*pe_done.tick((tag, "turn", g)))

            def ffn(tag, p0, t0, cols, last=False, fresh=None):
                if fresh is not None:
                    pe.wait_ge(*dve_done.at((fresh, "rstd")))
                for b in range(4):
                    m = pe.matmul(bank[b], zero[:, 0:P], zero[:], start=True, stop=True)

                def hidden(c, p, per, it, t, step, fresh=None):
                    hi, lo = open_panel(pe, p, per, it)
                    if t >= 2:
                        pe.wait_ge(hid_done, it * step + (t - 1))
                    for half in range(2):
                        v = [w_[:, 1024 * half:1024 * half + 1024].rearrange("p (k n) -> p k n", k=8) for w_ in (hi, lo)]
                        m = three(pe, bank[4 + c][:, S * half:S * half + S],
                                  [(v[0][:, k, :], v[1][:, k, :], xh[:, k, cols], xl[:, k, cols]) for k in range(8)],
                                  fresh=fresh if half == 0 else None)
                    m.then_inc(panel_used, 1)

                def output(p, per, it, pair_end, step, s_):
                    hi, lo = open_panel(pe, p, per, it)
                    pe.wait_ge(hid_hi, it * step + pair_end)
                    pe.wait_ge(hid_lo, it * step + pair_end)
                    for j in range(2):
                        for n in range(8):
                            w0 = 1024 * j + P * n
                            dst = bank[n // 2][:, S * (n % 2):S * (n % 2) + S]
                            pe.matmul(dst, hi[:, w0:w0 + P], hidh[:, s_, j, :], start=False, stop=False, skip_group_check=True)
                            pe.matmul(dst, hi[:, w0:w0 + P], hidl[:, s_, j, :], start=False, stop=False, skip_group_check=True)
                            m = pe.matmul(dst, lo[:, w0:w0 + P], hidh[:, s_, j, :], start=False, stop=False, skip_group_check=True)
                    m.then_inc(panel_used, 1)

                def body(p, per, it, t, step):
                    hidden(0, p, per, it, t, step)
                    hidden(1, p + 1, per, it, t + 1, step)
                    output(p + 2, per, it, t, step, 0)
                    hidden(0, p + 3, per, it, t + 2, step)
                    hidden(1, p + 4, per, it, t + 3, step)
                    output(p + 5, per, it, t + 2, step, 1)

                hidden(0, p0, 0, 0, t0, 0, fresh)
                hidden(1, p0 + 1, 0, 0, t0 + 1, 0)
                n = 4 if last else 5
                with repeat(pe, n) as it:
                    body(p0 + 2, 6, it, t0 + 2, 4)
                if last:
                    body(p0 + 2 + 24, 0, 0, t0 + 18, 0)
                output(p0 + 32, 0, 0, t0 + 22, 0, 0)

            site = [0]
            for l in range(L):
                stage(pe, "pe", ("mod", l), "load" if l == 0 else ("ffn", l - 1))
                p0 = base["mod", l]
                pe.wait_ge(*dve_done.at("c"))
                def mod_turn(p, per, it, taken):
                    for j in range(3):
                        hi, lo = open_panel(pe, p + j, per, it)
                        if taken is not None:
                            pe.wait_ge(mod_taken, it * 3 + taken + j)
                        for k in range(8):
                            wh, wl = hi[:, S * k:S * k + S], lo[:, S * k:S * k + S]
                            dst = bank[5 + j][0:2, 0:S]
                            pe.matmul(dst, ch[:, k, :], wh, start=k == 0, stop=False, skip_group_check=True)
                            pe.matmul(dst, ch[:, k, :], wl, start=False, stop=False, skip_group_check=True)
                            m = pe.matmul(dst, cl[:, k, :], wh, start=False, stop=k == 7, skip_group_check=True)
                        m.then_inc(panel_used, 1)

                def mod_rows(tiles, part):
                    for n in tiles:
                        m = pe.transpose(bank[4][:, 2 * n:2 * n + 2], modt[0:2, P * n:P * n + P], ident[0:2, 0:2])
                    m.then_inc(*pe_done.tick(("mod", l, "turn", part)))
                mod_turn(p0, 0, 0, 24 * l - 2 if l else None)
                with repeat(pe, 7) as it:
                    mod_turn(p0 + 3, 3, it, 24 * l + 1)
                pe.wait_ge(mod_taken, 24 * l + 24)
                mod_rows(range(16), 0)
                end("pe", ("mod", l))

                stage(pe, "pe", ("norm1", l), ("mod", l))
                mod_rows(range(16, 48), 1)
                pe_sum(pe, ("norm1", l), 8, 6, slice(0, T))
                end("pe", ("norm1", l))

                tg = ("mla", l)
                p0 = base["mla", l]
                TM = mix_tokens(l)
                g = generic_f(tg, p0, [(0, P), (P, P)], 8, 256, slice(0, TM), xh, xl, 0, fresh=("norm1", l))
                g = generic_f(tg, p0 + 1, [(0, P), (P, P)], 8, 256, slice(0, T), xh, xl, g)
                g = generic_f(tg, p0 + 2, [(0, P)], 8, P, slice(0, TM), xh, xl, g)
                g = generic_f(tg, p0 + 3, [(0, QH)], 8, QH, slice(0, T), xh, xl, g)
                pe.wait_ge(*dve_done.at((tg, "ev", 5)))
                pe.matmul(bank[7][0:QH, 0:S], const("rot1", QH)[:, 0:QH], kr[0:QH, 0:S], start=True, stop=True
                          ).then_inc(*pe_done.tick((tg, "krot")))
                for n, (name, k, nk_l, bk_, c_) in enumerate([("q", k, 3, 6, slice(0, TM)) for k in range(3)]
                                                             + [("kv", k, 2, 5, slice(0, T)) for k in range(2)]):
                    pe.wait_ge(*act_done.at(((tg, name), "sq", k)))
                    pe.matmul(bank[bk_][:, c_], ones[:], sq[:, n % 2, c_], start=k == 0, stop=k == nk_l - 1
                              ).then_inc(*pe_done.tick(((tg, name), "sum", k)))
                for j in range(3):
                    open_panel(pe, p0 + 4 + j)
                pe.wait_ge(*dve_done.at((tg, "lat ready")))
                for t in range(4):
                    dst = bank[t]
                    m = proj_t(p0 + 6, t, 2, kvh, kvl, dst.rearrange("p (h d) -> p h d", h=8),
                               lambda w_: (lambda k: w_[:, 1024 * k:1024 * k + 1024].rearrange("p (h n) -> p h n", h=8)[:, :, 64:128]))
                    m.then_inc(*pe_done.tick((tg, "v", t)))

                def mla_heads(hd):
                    if hd >= 1:
                        pe.wait_ge(*dve_done.at((tg, "qk", hd - 1)))
                    else:
                        pe.wait_ge(*dve_done.at((tg, "kr")))
                    m = proj_f(p0 + 4 + hd // 4, slice(0, TM), 384, QH * (hd % 4), QH, 3, qdh, qdl, bank[6][0:QH, 0:TM])
                    if hd % 4 == 3:
                        m.then_inc(panel_used, 1)
                    v = [w_[:, 0:2048].rearrange("p (k n) -> p k n", k=2)[:, :, P * hd:P * hd + 64] for w_ in (whi[(p0 + 6) % 3], wlo[(p0 + 6) % 3])]
                    m = three(pe, bank[7][0:64, :], [(v[0][:, k, :], v[1][:, k, :], kvh[:, k, :], kvl[:, k, :]) for k in range(2)])
                    if hd < HEADS - 1:
                        m.then_inc(*pe_done.tick((tg, "qk", hd)))
                    else:
                        m.then_inc(panel_used, 1)

                def mla_rot(hd):
                    pe.wait_ge(*act_done.at((tg, "q", hd)))
                    pe.matmul(bank[6][0:QH, 0:S], const("rot1", QH)[:, 0:QH], qt[0:QH, hd % 2, 0:S], start=True, stop=True
                              ).then_inc(*pe_done.tick((tg, "rot", hd)))

                raw_items = mla_items(l)
                per = len(raw_items) // HEADS
                pe.wait_ge(*dve_done.at((tg, "v", 3)))
                mla_heads(0)
                mla_rot(0)

                def prep(n):
                    hd = n // per
                    if n % per == 0:
                        pe.wait_ge(*dve_done.at((tg, "qk", hd)))
                        pe.wait_ge(*pool_done.at((tg, "krcopy", hd)))
                    if n % per == 1 and hd + 1 < HEADS:
                        mla_heads(hd + 1)
                        mla_rot(hd + 1)

                def mla_scores(hd, q, k0, nk):
                    return lambda b: pe.matmul(b[:, 0:nk], qt[0:QH, hd % 2, P * q:P * q + P], kt[0:QH, hd % 2, k0:k0 + nk],
                                               start=True, stop=True)
                items = [dict(nk=nk, dv=64, scores=mla_scores(hd, q, k0, nk), p=lambda j: pr[:, j % 2, :],
                              pt=lambda j: prt[:, j % 2, :],
                              v=[vtok[:, k0 // P + c, 64 * hd:64 * hd + 64] for c in range(nk // P)])
                         for hd, q, k0, nk in raw_items]
                attend(tg, items, prep)
                turn_y((tg, "y"), range(TM // P), lambda i: ytok[:, i, :])
                end("pe", tg)

                tg = ("gla", l)
                p0 = base["gla", l]
                stage(pe, "pe", tg, ("mla", l))
                g = generic_f(tg, p0, [(0, P), (P, P)], 8, 256, slice(0, T), xh, xl, 0)
                g = generic_f(tg, p0 + 1, [(0, P), (P, P)], 8, 256, slice(0, T), xh, xl, g)
                g = generic_t(tg, p0 + 2, range(4), g)
                g = generic_t(tg, p0 + 3, range(4), g)
                g = generic_f(tg, p0 + 4, [(0, 32)], 8, 32, slice(0, T), xh, xl, g)
                OT = TM // P
                for t in range(OT):
                    pe.matmul(bank[t], zero[:, 0:P], zero[:], start=True, stop=True)
                pe.wait_ge(*dve_done.at((tg, "ev", g - 1)))
                pe.wait_ge(*loaded2.at(("wg", l)))
                pe.wait_ge(*pool_done.at((tg, "ones")))
                for t in range(4):
                    if t >= 2:
                        pe.wait_ge(*dve_done.at((tg, "negabs", t - 2)))
                    pe.matmul(bank[4 + t % 2], lr[0:33, P * t:P * t + P], wg[0:33, :], start=True, stop=True
                              ).then_inc(*pe_done.tick((tg, "z", t)))
                    if t >= 2:
                        pe.wait_ge(*dve_done.at((tg, "ktok", t - 2)))
                    for f in range(2):
                        m = pe.transpose(bank[6 + t % 2][:, f * P:(f + 1) * P], gk[:, f, P * t:P * t + P], ident)
                    m.then_inc(*pe_done.tick((tg, "ktok", t)))
                for d, dn in enumerate("fb"):
                    dt_ = (tg, dn)
                    pe.wait_ge(*dve_done.at((tg, "ktok", 3)))
                    pe.wait_ge(*dve_done.at((tg, "la", 3)))
                    if d:
                        pe.wait_ge(*dve_done.at(((tg, "f"), "end")))
                        pe.wait_ge(*act_done.at(((tg, "f"), "rem", 3)))
                    for f in range(2):
                        for t in range(4):
                            m = pe.matmul(bank[4 + f][:, P * t:P * t + P], la[:, t, S * d + P * f:S * d + P * f + P],
                                          const("tri_" + dn), start=True, stop=True)
                        m.then_inc(*pe_done.tick((dt_, "cum", f)))
                    for t in range(4):
                        if t >= 2:
                            pe.wait_ge(*act_done.at((dt_, "rem", t - 2)))
                        pe.matmul(bank[6 + t % 2][:, 0:S], const("strict_" + dn), la[:, t, S * d:S * d + S],
                                  start=True, stop=True).then_inc(*pe_done.tick((dt_, "rem", t)))
                    pe.wait_ge(*dve_done.at((dt_, "kinv")))
                    pe.wait_ge(*act_done.at((dt_, "expn", 1)))

                    def within(t):
                        if t == 1:
                            pe.wait_ge(*act_done.at((dt_, "rem", 3)))
                        elif t >= 2:
                            pe.wait_ge(*dve_done.at((dt_, "att", t - 2)))
                        for hd in range(4):
                            b0 = 64 * (hd % 2)
                            m = pe.matmul(bank[4 + 2 * (t % 2) + hd % 2][:, P * (hd // 2):P * (hd // 2) + P],
                                          kinv[b0:b0 + 64, hd // 2, P * t:P * t + P],
                                          qdec[b0:b0 + 64, hd // 2, P * t:P * t + P], start=True, stop=True)
                        m.then_inc(*pe_done.tick((dt_, "att", t)))
                    within(0)
                    for t in range(OT):
                        if t + 1 < OT:
                            within(t + 1)
                        pe.wait_ge(*dve_done.at((dt_, "att", t)))
                        for hd in range(4):
                            m = pe.matmul(bank[t][:, P * hd:P * hd + P], attm[:, t % 2, P * hd:P * hd + P],
                                          gv[:, t, P * hd:P * hd + P], start=False, stop=False, skip_group_check=True)
                        m.then_inc(*pe_done.tick((dt_, "intra", t)))
                    order = [4, 5, 6, 7, 0, 1, 2, 3] if d == 0 else [7, 6, 5, 4, 3, 2, 1, 0]

                    def outer(n):
                        t, r = order[n] // 2, 64 * (order[n] % 2)
                        for hd in range(4):
                            b0 = 64 * (hd % 2)
                            m = pe.matmul(bank[4 + n % 2][b0:b0 + 64, P * (hd // 2):P * (hd // 2) + P],
                                          kend[r:r + 64, t, 64 * hd:64 * hd + 64], gv[r:r + 64, t, P * hd:P * hd + P],
                                          start=True, stop=True)
                        m.then_inc(*pe_done.tick((dt_, "kv", n)))

                    def gate(i, j):
                        if i == 0:
                            open_panel(pe, p0 + 5 + j)
                        if i >= 2 and j == 0:
                            pe.wait_ge(*act_done.at((tg, "silu", i - 2)))
                        m = proj_t(p0 + 5 + j, i, 8, xh, xl, bank[6 + i % 2][:, 256 * j:256 * j + 256],
                                   lambda w_: (lambda k: w_[:, 256 * k:256 * k + 256]))
                        if i == OT - 1:
                            m.then_inc(panel_used, 1)
                        elif j:
                            m.then_inc(*pe_done.tick((tg, "gate", i)))
                    pe.wait_ge(*dve_done.at((dt_, "kend", 3)))
                    outer(0)
                    for n, chunk in enumerate(order):
                        t, r = chunk // 2, 64 * (chunk % 2)
                        if n < 6:
                            if n:
                                pe.wait_ge(*dve_done.at((dt_, "state", n - 1)))
                            outer(n + 1)
                        if d and n < 2 * OT:
                            gate(n // 2, n % 2)
                        if n:
                            pe.wait_ge(*dve_done.at((dt_, "state", n - 1)))
                        if t < OT and n:
                            for f in range(2):
                                m = pe.matmul(bank[t][r:r + 64, S * f:S * f + S], qdec[:, f, 64 * chunk:64 * chunk + 64],
                                              state[:, n % 2, f, :], start=False, stop=False, skip_group_check=True)
                            m.then_inc(*pe_done.tick((dt_, "from state", n)))
                        else:
                            pe_done.mark((dt_, "from state", n))
                pe.wait_ge(*act_done.at((tg, "silu", OT - 1)))
                turn_y((tg, "y"), range(OT), lambda i: gv[:, i, :])
                end("pe", tg)

                tg = ("na", l)
                p0 = base["na", l]
                stage(pe, "pe", tg, ("gla", l))
                g = 0
                for j in range(2):
                    g = generic_f(tg, p0 + j, [(0, P), (P, P)], 8, 256, slice(0, TM), xh, xl, g)
                for j in range(2):
                    g = generic_f(tg, p0 + 2 + j, [(0, P), (P, P)], 8, 256, slice(0, T), xh, xl, g)
                for j in range(2):
                    g = generic_t(tg, p0 + 4 + j, range(4), g)
                pe.wait_ge(*dve_done.at((tg, "ev", g - 1)))

                def na_scores(hd, q, k0, nk):
                    b0 = 64 * (hd % 2)
                    return lambda b: pe.matmul(b[:, 0:nk], nq[b0:b0 + 64, hd // 2, P * q:P * q + P],
                                               nk_[b0:b0 + 64, hd // 2, k0:k0 + nk], start=True, stop=True)
                nk_ = nk
                na_list = sorted(raw_items, key=lambda x: (x[1], x[0]))
                items = [dict(nk=n_, dv=64, scores=na_scores(hd, q, k0, n_), p=lambda j: npr[:, j % 2, :],
                              pt=lambda j: nprt[:, j % 2, :],
                              v=[nv[:, k0 // P + c, 64 * hd:64 * hd + 64] for c in range(n_ // P)])
                         for hd, q, k0, n_ in na_list]

                def na_prep(n):
                    if n % HEADS == 3 and n >= HEADS:
                        turn_na(n // HEADS - 1)

                def turn_na(i):
                    if i >= 1:
                        pe.wait_ge(*act_done.at((tg, "turned", i - 1)))
                    pe.wait_ge(*dve_done.at((tg, "y", HEADS * i + HEADS - 1)))
                    for c in range(4):
                        m = pe.transpose(bank[6][:, c * P:(c + 1) * P], nytok[:, 0, c * P:(c + 1) * P], ident)
                    m.then_inc(*pe_done.tick((tg, "turn", i)))
                attend(tg, items, na_prep)
                turn_na(OT - 1)
                end("pe", tg)

                tg = ("merge", l)
                p0 = base["merge", l]
                stage(pe, "pe", tg, ("na", l))
                pe.wait_ge(*dve_done.at((tg, "yl")))
                m0 = 8 * l
                with repeat(pe, 8) as it:
                    hi, lo = open_panel(pe, p0, 3, it)
                    pe.wait_ge(gate_ready, it * 3 + 3 * m0)

                    def gate(c0, b, hi, lo):
                        return three(pe, bank[b][:, 0:TM], [(hi[:, c0 + P * k:c0 + P * k + P], lo[:, c0 + P * k:c0 + P * k + P],
                                                             xh[:, k, 0:TM], xl[:, k, 0:TM]) for k in range(8)])

                    def branch(c0, b, k0, hi, lo):
                        return three(pe, bank[b][:, 0:TM], [(hi[:, c0 + P * k:c0 + P * k + P], lo[:, c0 + P * k:c0 + P * k + P],
                                                             yh[:, k0 + k, 0:TM], yl[:, k0 + k, 0:TM]) for k in range(4)])
                    gate(0, 0, hi, lo)
                    gate(1024, 1, hi, lo).then_inc(panel_used, 1)
                    hi, lo = open_panel(pe, p0 + 1, 3, it)
                    gate(0, 2, hi, lo)
                    pe.wait_ge(merged, it + m0)
                    branch(1024, 3, 0, hi, lo)
                    branch(1536, 4, 4, hi, lo).then_inc(panel_used, 1)
                    hi, lo = open_panel(pe, p0 + 2, 3, it)
                    branch(0, 5, 8, hi, lo).then_inc(panel_used, 1)
                end("pe", tg)

                tg = ("out", l)
                stage(pe, "pe", tg, ("merge", l))
                pe.wait_ge(*dve_done.at((tg, "ml")))
                g = 0
                for j in range(4):
                    g = generic_f(tg, base[tg] + j, [(0, P), (P, P)], 8, 256, slice(0, TM), xh, xl, g)
                end("pe", tg)

                stage(pe, "pe", ("norm2", l), ("out", l))
                pe_sum(pe, ("norm2", l), 8, 6, slice(0, TM))
                end("pe", ("norm2", l))

                for part in range(TM // S):
                    tg = ("ffn", l, part)
                    if part:
                        stage(pe, "pe", tg, ("ffn", l, part - 1))
                    ffn(tg, base[tg], FT * site[0], KINDS[part][1], fresh=("norm2", l) if part == 0 else None)
                    site[0] += 1
                    end("pe", tg)
                end("pe", ("ffn", l))

            stage(pe, "pe", "block2", ("ffn", L - 1))
            pe_sum(pe, "final", 8, 6, slice(0, S))
            end("pe", "block2")
            prev = "block2"

            def layer_norm_pe(tg):
                for k in range(8):
                    pe.wait_ge(*dve_done.at((tg, "u", k)))
                    pe.matmul(bank[ln_bank(tg)][:, 0:S], ones[:], h[:, k, 0:S], start=k == 0, stop=k == 7
                              ).then_inc(*pe_done.tick((tg, "mean", k)))
                pe_sum(pe, tg, 8, ln_bank(tg) + 1, slice(0, S))

            for l in range(L):
                for which in (1, 2):
                    if which == 2:
                        tg = ("win2", l)
                        p0 = base[tg]
                        g = 0
                        for j in range(4):
                            g = generic_f(tg, p0 + j, [(0, P), (P, P)], 8, 256, slice(0, S), xh, xl, g, fresh=prev if j == 0 else None)
                        for j in range(2):
                            g = generic_t(tg, p0 + 4 + j, range(2), g)
                        for j in range(2):
                            g = generic_f(tg, p0 + 6 + j, [(0, P), (P, P)], 8, 256, slice(0, S), xh, xl, g)
                        open_panel(pe, p0 + 8)
                        pe.wait_ge(*dve_done.at((tg, "ev", g - 4)))
                        m = proj_f(p0 + 8, slice(0, S), 256, 0, P, 8, xh, xl, bank[4 + g % 4][:, 0:S])
                        m.then_inc(*pe_done.tick((tg, "mm", g)))
                        g += 1
                        for t in range(2):
                            pe.wait_ge(*dve_done.at((tg, "ev", g - 4)))
                            m = proj_t(p0 + 8, t, 8, xh, xl, bank[4 + g % 4][:, 0:P],
                                       lambda w_: (lambda k: w_[:, 256 * k + P:256 * k + 256]))
                            if t == 1:
                                m.then_inc(panel_used, 1)
                            else:
                                m.then_inc(*pe_done.tick((tg, "mm", g)))
                            g += 1
                        for i in range(13):
                            if i >= 2:
                                pe.wait_ge(*dve_done.at((tg, "roped", i - 2)))
                            elif i == 0:
                                pe.wait_ge(*dve_done.at((tg, "ev", g - 1)))
                            pe.matmul(bank[i % 2][:, 0:S], const2("rot2"), f2[:, i, :], start=True, stop=True
                                      ).then_inc(*pe_done.tick((tg, "rot", i)))
                        pe.wait_ge(*dve_done.at((tg, "roped", 12)))
                        pe.matmul(bank[2][:, 0:S], const2("swap"), f2[:, 12, :], start=True, stop=True
                                  ).then_inc(*pe_done.tick((tg, "swap")))
                        pe.wait_ge(*dve_done.at((tg, "swap")))
                        end("pe", tg)
                        prev = tg
                        tg = ("att2", l)
                        stage(pe, "pe", tg, prev)

                        def diff_scores(hd, q):
                            def run(b, b2):
                                for c in range(2):
                                    m = pe.matmul((b, b2)[c][:, 0:S], f2[64 * c:64 * c + 64, hd, P * q:P * q + P],
                                                  f2[64 * c:64 * c + 64, 4 + hd, :], start=True, stop=True)
                                return m
                            return run

                        def swa_scores(hd, q):
                            b0 = 64 * (hd % 2)
                            key = 12 if hd // 4 == hd % 2 else 13
                            return lambda b: pe.matmul(b[:, 0:S], f2[b0:b0 + 64, 8 + hd // 2, P * q:P * q + P],
                                                       f2[b0:b0 + 64, key, :], start=True, stop=True)
                        items = [dict(nk=S, dv=P, diff=True, scores=diff_scores(hd, q), p=lambda j: ap_[:, j % 2, :],
                                      pt=lambda j: apt[:, j % 2, :], v=[dvt[:, c, P * hd:P * hd + P] for c in range(2)])
                                 for hd in range(4) for q in range(2)]
                        items += [dict(nk=S, dv=64, scores=swa_scores(hd, q), p=lambda j: ap_[:, j % 2, :],
                                       pt=lambda j: apt[:, j % 2, :],
                                       v=[dvt[:, c, 512 + 64 * (hd // 4):576 + 64 * (hd // 4)] for c in range(2)])
                                  for hd in range(8) for q in range(2)]
                        attend(tg, items, lambda n: None)
                        turn_y((tg, "y"), range(2), lambda i: ytok2[:, i, :], n_tiles=8)
                        end("pe", tg)
                        tg = ("out2", l)
                        stage(pe, "pe", tg, ("att2", l))
                        pe.wait_ge(*dve_done.at((tg, "ml")))
                        g = 0
                        for j in range(4):
                            g = generic_f(tg, base[tg] + j, [(0, P), (P, P)], 8, 256, slice(0, S), xh, xl, g)
                        layer_norm_pe(tg)
                        end("pe", tg)
                        prev = tg
                    tg = ("ffn%d" % which, l)
                    ffn(tg, base[tg], FT * site[0], slice(0, S), last=which == 2 and l == L - 1,
                        fresh=prev if prev != "block2" else "final")
                    site[0] += 1
                    layer_norm_pe(tg)
                    end("pe", tg)
                    prev = tg
            for b in range(2):
                for t in range(2):
                    for c in range(4):
                        if t == 0:
                            pe.wait_ge(*act_done.at((prev, "hi", 4 * b + c)))
                        m = pe.transpose(bank[2 * t + b][:, c * P:(c + 1) * P], h[:, 4 * b + c, P * t:P * t + P], ident)
                    m.then_inc(*pe_done.tick(("oT", 2 * t + b)))
            end("pe", "store")

        def product(eng, tag, p, i, n, g):
            if i == n - 1:
                eng.wait_ge(panel_used, p + 1)
            else:
                eng.wait_ge(*pe_done.at((tag, "mm", g)))

        @block.scalar
        def _(act):
            def step(p, per=0, it=0, turns=1):
                split_act(act, p + 2, per, it, turns)

            act.wait_ge(*pool_done.at("setup"))
            act.wait_ge(*dve_done.at("par"))
            act.activation(sq[:, 0, 0:16], par[:, 0:16], ACT.Silu).then_inc(*act_done.tick("silu c"))
            act.wait_ge(*act_done.at("silu c"))
            for v in range(2):
                m = act.activation(ch[:, :, v], sq[:, 0, 8 * v:8 * v + 8], ACT.Copy)
            m.then_inc(*act_done.tick("ch"))
            end("act", "load")
            split_act(act, 0)
            split_act(act, 1)

            def norm_hi(tag, nk, src, dst, parts, rdy):
                for k in range(nk):
                    act.wait_ge(*dve_done.at((tag, "t", k)))
                    for cols, bias in parts(k):
                        if bias is None:
                            m = act.activation(dst(k, cols), src(k, cols), ACT.Copy)
                        else:
                            m = act.activation(dst(k, cols), src(k, cols), ACT.Identity, bias=bias)
                    m.then_inc(*act_done.tick((tag, "hi", k)))

            def attend(tag, items, hooks=lambda n: None):
                N = len(items)
                for n in range(N + 2):
                    if n < N:
                        hooks(n)
                        it_ = items[n]
                        act.wait_ge(*dve_done.at((tag, "max", n)))
                        if it_.get("diff"):
                            if n >= 2:
                                act.wait_ge(*dve_done.at((tag, "exp", n - 2)))
                            for c in range(2):
                                m = act.activation(it_["e"](n)[:, S * c:S * c + S], score_banks(n)[c][:, 0:S], ACT.Exp,
                                                   bias=it_["st"](n, c), accum_out=it_["st"](n, 2 + c))
                        else:
                            if n >= 2:
                                act.wait_ge(*pe_done.at((tag, "t", n - 2)))
                            m = act.activation(it_["p"](n), score_banks(n)[0][:, 0:it_["nk"]], ACT.Exp,
                                               bias=it_["st"](n, 0), accum_out=it_["st"](n, 2))
                        m.then_inc(*act_done.tick((tag, "exp", n)))
                        if it_.get("sink") is not None:
                            act.activation(it_["st"](n, 3), it_["sink"], ACT.Exp, bias=it_["st"](n, 0)
                                           ).then_inc(*act_done.tick((tag, "sink", n)))
                    if n >= 2:
                        j = n - 2
                        act.wait_ge(*pe_done.at((tag, "t", j)))
                        if j >= 2:
                            act.wait_ge(*pe_done.at((tag, "o", j - 2)))
                        act.activation(items[j]["pt"](j), turned_at(tag, j, items[j]["nk"]), ACT.Copy
                                       ).then_inc(*act_done.tick((tag, "pt", j)))

            def ffn(tag, p0, t0, last=False):
                def hidden(c, p, per, it, t, nstep, s_, turns):
                    step(p, per, it, turns)
                    act.wait_ge(panel_used, it * per + (p + 1))
                    if t >= 2:
                        act.wait_ge(hid_done, it * nstep + (t - 1))
                    act.activation(sg[:, c, :], bank[4 + c][:, 0:S], ACT.Silu).then_inc(silu_done, 1)
                    act.wait_ge(hid_done, it * nstep + (t + 1))
                    act.activation(hidh[:, s_, c, :], hidf[:, c, :], ACT.Copy).then_inc(hid_hi, 1)

                def body(p, per, it, t, nstep, turns):
                    for half in range(2):
                        hidden(0, p + 3 * half, per, it, t + 2 * half, nstep, 1 - half, turns)
                        hidden(1, p + 1 + 3 * half, per, it, t + 1 + 2 * half, nstep, 1 - half, turns)
                        step(p + 2 + 3 * half, per, it, turns)
                hidden(0, p0, 0, 0, t0, 0, 0, 1)
                hidden(1, p0 + 1, 0, 0, t0 + 1, 0, 0, 1)
                n = 4 if last else 5
                with repeat(act, n) as it:
                    body(p0 + 2, 6, it, t0 + 2, 4, n)
                if last:
                    body(p0 + 26, 0, 0, t0 + 18, 0, 1)
                step(p0 + 32)

            site = [0]
            for l in range(L):
                stage(act, "act", ("mod", l), "load" if l == 0 else ("ffn", l - 1))
                p0 = base["mod", l]
                for j in range(3):
                    step(p0 + j)
                with repeat(act, 7) as it:
                    for j in range(3):
                        step(p0 + 3 + j, 3, it, 7)
                end("act", ("mod", l))

                tg = ("norm1", l)
                stage(act, "act", tg, ("mod", l))
                act_squares(act, tg, [h[:, k, :] for k in range(8)], slice(0, T), 0, D, 6, lambda k: None)
                norm_hi(tg, 8, lambda k, c: h_n[:, k % 3, c], lambda k, c: xh[:, k, c],
                        lambda k: [(c, mod[:, 2 * l + kind, k:k + 1]) for kind, c in KINDS], None)
                end("act", tg)

                tg = ("mla", l)
                p0 = base["mla", l]
                stage(act, "act", tg, ("norm1", l))
                TM = mix_tokens(l)
                OT = TM // P
                for j in range(5):
                    step(p0 + j)
                norms = (("q", 3, slice(0, TM), 0, 6, qdh, stat), ("kv", 2, slice(0, T), 3, 5, kvh, stat2))
                act.wait_ge(*dve_done.at((tg, "ev", 5)))
                squares = [("q", 0), ("q", 1), ("q", 2), ("kv", 0), ("kv", 1)]
                for n, (name, k) in enumerate(squares):
                    _, _, c_, off, _, _, _ = norms[name == "kv"]
                    if n >= 2:
                        before, k_ = squares[n - 2]
                        act.wait_ge(*pe_done.at(((tg, before), "sum", k_)))
                    act.activation(sq[:, n % 2, c_], downs[:, off + k, c_], ACT.Square).then_inc(*act_done.tick(((tg, name), "sq", k)))
                for name, n_, c_, off, bk, dst, st_ in norms:
                    act.wait_ge(*pe_done.at(((tg, name), "sum", n_ - 1)))
                    act.activation(st_[:, c_], bank[bk][:, c_], ACT.Sqrt, bias=eps[:, 0:1],
                                   scale=1.0 / (P * n_)).then_inc(*act_done.tick(((tg, name), "std")))
                for name, n_, c_, off, bk, dst, st_ in norms:
                    for k in range(n_):
                        act.wait_ge(*dve_done.at(((tg, name), "t", k)))
                        act.activation(dst[:, k, c_], downs[:, off + k, c_], ACT.Copy).then_inc(*act_done.tick(((tg, name), "hi", k)))
                raw_items = mla_items(l)
                per = len(raw_items) // HEADS

                def q_evac(hd):
                    if hd < HEADS - 1:
                        act.wait_ge(*pe_done.at((tg, "qk", hd)))
                    else:
                        act.wait_ge(panel_used, p0 + 7)
                    act.activation(qt[0:QH, hd % 2, 0:TM], bank[6][0:QH, 0:TM], ACT.Copy, scale=MLA_SCALE
                                   ).then_inc(*act_done.tick((tg, "q", hd)))
                act.wait_ge(*dve_done.at((tg, "lat ready")))
                q_evac(0)

                def hook(n):
                    if n % per == 1 and n // per + 1 < HEADS:
                        q_evac(n // per + 1)
                        if n // per + 1 == 4:
                            step(p0 + 5)
                items = [dict(nk=n_, p=lambda j, n_=n_: pr[:, j % 2, 0:n_], pt=lambda j, n_=n_: prt[:, j % 2, 0:n_],
                              st=lambda j, c: st8[:, 4 * (j % 4) + c:4 * (j % 4) + c + 1]) for _, _, _, n_ in raw_items]
                attend(tg, items, hook)
                step(p0 + 6)
                end("act", tg)

                tg = ("gla", l)
                p0 = base["gla", l]
                stage(act, "act", tg, ("mla", l))
                for j in range(5):
                    step(p0 + j)
                for t in range(4):
                    act.wait_ge(*dve_done.at((tg, "negabs", t)))
                    act.activation(ez[:, t, :], ez[:, t, :], ACT.Exp).then_inc(*act_done.tick((tg, "zexp", t)))
                for t in range(4):
                    act.wait_ge(*act_done.at((tg, "zexp", t)))
                    act.activation(ez[:, t, :], ez[:, t, :], ACT.Ln, bias=1.0).then_inc(*act_done.tick((tg, "ln", t)))
                for d, dn in enumerate("fb"):
                    dt_ = (tg, dn)
                    if d:
                        act.wait_ge(*dve_done.at(((tg, "f"), "end")))
                        act.wait_ge(*pe_done.at(((tg, "f"), "from state", 7)))
                    for f in range(2):
                        act.wait_ge(*pe_done.at((dt_, "cum", f)))
                        act.activation(expc[:, f, :], bank[4 + f], ACT.Exp).then_inc(*act_done.tick((dt_, "expp", f)))
                        act.activation(kinv[:, f, :], bank[4 + f], ACT.Exp, scale=-1.0).then_inc(*act_done.tick((dt_, "expn", f)))
                    for t in range(4):
                        act.wait_ge(*pe_done.at((dt_, "rem", t)))
                        act.activation(kend[:, t, :], bank[6 + t % 2][:, 0:S], ACT.Exp).then_inc(*act_done.tick((dt_, "rem", t)))
                for i in range(OT):
                    if i < OT - 1:
                        act.wait_ge(*pe_done.at((tg, "gate", i)))
                    else:
                        act.wait_ge(panel_used, p0 + 7)
                    act.activation(la[:, i, :], bank[6 + i % 2], ACT.Silu).then_inc(*act_done.tick((tg, "silu", i)))
                act.wait_ge(*pe_done.at(((tg, "b"), "from state", 7)))
                act.wait_ge(*dve_done.at(((tg, "b"), "end")))
                for i in range(OT):
                    if i:
                        act.wait_ge(*act_done.at((tg, "ss", i - 1, 3)))
                    for hd in range(4):
                        act.activation(expc[:, 0, P * hd:P * hd + P], bank[i][:, P * hd:P * hd + P], ACT.Square,
                                       accum_out=gst[:, 4 * i + hd:4 * i + hd + 1]).then_inc(*act_done.tick((tg, "ss", i, hd)))
                act.wait_ge(*act_done.at((tg, "ss", OT - 1, 3)))
                act.activation(gst[:, 0:4 * OT], gst[:, 0:4 * OT], ACT.Sqrt, bias=eps[:, 0:1], scale=1.0 / P
                               ).then_inc(*act_done.tick((tg, "gstd")))
                step(p0 + 5)
                step(p0 + 6)
                end("act", tg)

                tg = ("na", l)
                p0 = base["na", l]
                stage(act, "act", tg, ("gla", l))
                for j in range(6):
                    step(p0 + j)
                na_list = sorted(raw_items, key=lambda x: (x[1], x[0]))

                def turned(i):
                    act.wait_ge(*pe_done.at((tg, "turn", i)))
                    act.activation(y[:, 8:12, P * i:P * i + P], bank[6].rearrange("p (c n) -> p c n", c=4), ACT.Copy
                                   ).then_inc(*act_done.tick((tg, "turned", i)))

                def na_hook(n):
                    if n % HEADS == 5 and n >= HEADS:
                        turned(n // HEADS - 1)
                items = [dict(nk=n_, p=lambda j, n_=n_: npr[:, j % 2, 0:n_], pt=lambda j, n_=n_: nprt[:, j % 2, 0:n_],
                              st=lambda j, c: nst[:, 4 * (j % 4) + c:4 * (j % 4) + c + 1]) for _, _, _, n_ in na_list]
                attend(tg, items, na_hook)
                turned(OT - 1)
                end("act", tg)

                tg = ("merge", l)
                p0 = base["merge", l]
                stage(act, "act", tg, ("na", l))
                for k in range(12):
                    m = act.activation(yh[:, k, 0:TM], y[:, k, 0:TM], ACT.Copy)
                    m.then_inc(*act_done.tick((tg, "yh", k)))
                m0 = 8 * l
                with repeat(act, 8) as it:
                    for j in range(3):
                        step(p0 + j, 3, it, 8)
                        if j == 0:
                            act.wait_ge(panel_used, it * 3 + (p0 + 1))
                            act.wait_ge(merged, it + m0)
                            for b in range(2):
                                act.activation(gates[:, b, 0:TM], bank[b][:, 0:TM], ACT.Sigmoid).then_inc(gate_ready, 1)
                        if j == 1:
                            act.wait_ge(panel_used, it * 3 + (p0 + 2))
                            act.activation(gates[:, 2, 0:TM], bank[2][:, 0:TM], ACT.Sigmoid).then_inc(gate_ready, 1)
                end("act", tg)

                tg = ("out", l)
                stage(act, "act", tg, ("merge", l))
                act.wait_ge(merged, 8 * (l + 1))
                act.wait_ge(panel_used, base[tg])
                for k in range(8):
                    act.activation(xh[:, k, 0:TM], mf[:, k, 0:TM], ACT.Copy).then_inc(*act_done.tick((tg, "mh", k)))
                for j in range(4):
                    step(base[tg] + j)
                end("act", tg)

                tg = ("norm2", l)
                stage(act, "act", tg, ("out", l))
                act_squares(act, tg, [h[:, k, 0:TM] for k in range(8)], slice(0, TM), 0, D, 6, lambda k: None)
                norm_hi(tg, 8, lambda k, c: h_n[:, k % 3, c], lambda k, c: xh[:, k, c],
                        lambda k: [(c, mod[:, 2 * l + kind, 24 + k:25 + k]) for kind, c in KINDS[:TM // S]], None)
                end("act", tg)
                for part in range(TM // S):
                    tg = ("ffn", l, part)
                    stage(act, "act", tg, ("norm2", l) if part == 0 else ("ffn", l, part - 1))
                    ffn(tg, base[tg], FT * site[0])
                    site[0] += 1
                    end("act", tg)
                end("act", ("ffn", l))

            stage(act, "act", "block2", ("ffn", L - 1))
            act_squares(act, "final", [h[:, k, 0:S] for k in range(8)], slice(0, S), 0, D, 6, lambda k: None)
            for k in range(8):
                act.wait_ge(*dve_done.at(("final", "t", k)))
                act.activation(xh[:, k, 0:S], h[:, k, 0:S], ACT.Copy).then_inc(*act_done.tick(("final", "hi", k)))
            for n, dst in ((0, sin2), (1, cos2)):
                act.wait_ge(*dve_done.at(("angle", n)))
                act.activation(dst[:], ang[:, n, :], ACT.Sin).then_inc(*act_done.tick(("trig", n)))
            act.wait_ge(*dve_done.at("lam dots"))
            act.activation(ast[:, 0:2 * L], ast[:, 0:2 * L], ACT.Exp).then_inc(*act_done.tick("lam exp"))
            end("act", "block2")
            prev = "block2"

            def layer_norm_act(tg, last=False):
                act.wait_ge(*pe_done.at((tg, "mean", 7)))
                act.activation(rtmp[:, 0, :], bank[ln_bank(tg)][:, 0:S], ACT.Copy, scale=1.0 / D
                               ).then_inc(*act_done.tick((tg, "mean")))
                act_squares(act, tg, [h[:, k, 0:S] for k in range(8)], slice(0, S), 1 if tg[0] == "out2" else 2, D, ln_bank(tg) + 1,
                            lambda k: act.wait_ge(*dve_done.at((tg, "d", k))))
                for k in range(8):
                    act.wait_ge(*dve_done.at((tg, "t", k)))
                    dst = h if last else xh
                    act.activation(dst[:, k, 0:S], h[:, k, 0:S], ACT.Identity, bias=col("ln_b_2", ln_col(tg) + k)
                                   ).then_inc(*act_done.tick((tg, "hi", k)))

            for l in range(L):
                for which in (1, 2):
                    if which == 2:
                        tg = ("win2", l)
                        stage(act, "act", tg, prev)
                        for j in range(9):
                            step(base[tg] + j)
                        end("act", tg)
                        tg = ("att2", l)
                        stage(act, "act", tg, ("win2", l))
                        items = [dict(nk=S, diff=True, p=lambda j: ap_[:, j % 2, 0:S], e=lambda j: ap_[:, j % 2, :],
                                      pt=lambda j: apt[:, j % 2, :], st=lambda j, c: ast[:, 4 * (j % 4) + c:4 * (j % 4) + c + 1])
                                 for _ in range(8)]
                        items = [dict(i_, e=lambda j: prd(j)) for i_ in items]
                        items += [dict(nk=S, p=lambda j: ap_[:, j % 2, 0:S], pt=lambda j: apt[:, j % 2, :], sink=sink[:, l, hd:hd + 1],
                                       st=lambda j, c: ast[:, 4 * (j % 4) + c:4 * (j % 4) + c + 1])
                                  for hd in range(8) for _ in range(2)]
                        attend(tg, items)
                        act.wait_ge(*dve_done.at((tg, "y", 7)))
                        for i in range(2):
                            for hd in range(4):
                                if i or hd:
                                    act.wait_ge(*act_done.at((tg, "ss", i, hd - 1) if hd else (tg, "ss", 0, 3)))
                                act.activation(rtmp[:, 0, 0:P], ytok2[:, i, P * hd:P * hd + P], ACT.Square,
                                               accum_out=ast[:, 16 + 4 * i + hd:17 + 4 * i + hd]).then_inc(*act_done.tick((tg, "ss", i, hd)))
                        act.wait_ge(*act_done.at((tg, "ss", 1, 3)))
                        act.activation(ast[:, 16:24], ast[:, 16:24], ACT.Sqrt, bias=eps[:, 1:2], scale=1.0 / P
                                       ).then_inc(*act_done.tick((tg, "std")))
                        for i in range(2):
                            for b in range(2):
                                g = 2 * i + b
                                act.wait_ge(*pe_done.at(((tg, "y"), "turn", g)))
                                act.activation(xh[:, 4 * b:4 * b + 4, P * i:P * i + P], bank[6 + g % 2].rearrange("p (c n) -> p c n", c=4),
                                               ACT.Copy).then_inc(*act_done.tick((tg, "turned hi", g)))
                        end("act", tg)
                        tg = ("out2", l)
                        stage(act, "act", tg, ("att2", l))
                        for j in range(4):
                            step(base[tg] + j)
                        layer_norm_act(tg)
                        end("act", tg)
                        prev = tg
                    tg = ("ffn%d" % which, l)
                    stage(act, "act", tg, prev)
                    last = which == 2 and l == L - 1
                    ffn(tg, base[tg], FT * site[0], last)
                    site[0] += 1
                    layer_norm_act(tg, last)
                    end("act", tg)
                    prev = tg
            stage(act, "act", "store", prev)
            end("act", "store")

        @block.vector
        def _(dve):
            def step(p, per=0, it=0, turns=1):
                split_dve(dve, p + 2, per, it, turns)

            dve.wait_ge(*pool_done.at("setup"))
            for g in range(8):
                t, half = g // 2, g % 2
                dve.wait_ge(*pe_done.at(("xT", g)))
                dve.tensor_copy(h[:, 4 * half:4 * half + 4, P * t:P * t + P], bank[g].rearrange("p (c n) -> p c n", c=4)
                                ).then_inc(*dve_done.tick(("xT", g)))
            dve.wait_ge(*pe_done.at("par"))
            dve.tensor_copy(par[:, 0:P], bank[0][:, 0:P])
            dve.tensor_copy(par[:, P:P + 82], bank[0][:, P:P + 82])
            dve.tensor_copy(par[:, P + 82:P + 130], bank[0][:, 2 * P:2 * P + 48]).then_inc(*dve_done.tick("par"))
            dve.wait_ge(*act_done.at("ch"))
            for v in range(2):
                m = dve.tensor_tensor(cl[:, :, v], sq[:, 0, 8 * v:8 * v + 8], ch[:, :, v].bitcast(F32), ALU.subtract)
            m.then_inc(*dve_done.tick("c"))
            end("dve", "load")
            split_dve(dve, 0)
            split_dve(dve, 1)

            def modulated_norm(tg, l, tile0, cols_n):
                w = "norm1_w" if tile0 == 0 else "norm2_w"
                for v in range(2):
                    m = dve.scalar_tensor_tensor(mul[:, v, :], mod[:, 2 * l + v, tile0 + 8:tile0 + 16], 1.0,
                                                 par[:, PAR[w][0] + 8 * l:PAR[w][0] + 8 * l + 8], ALU.add, ALU.mult)
                m.then_inc(*dve_done.tick((tg, "mul")))
                dve.wait_ge(*dve_done.at((tg, "mul")))
                dve_rstd(dve, tg, slice(0, cols_n))
                for k in range(9):
                    if k < 8:
                        if k >= 3:
                            dve.wait_ge(*dve_done.at((tg, "lo", k - 3)))
                        for kind, c in KINDS[:cols_n // S]:
                            m = dve.scalar_tensor_tensor(h_n[:, k % 3, c], h[:, k, c], mul[:, kind, k:k + 1], stat[:, c],
                                                         ALU.mult, ALU.mult)
                        m.then_inc(*dve_done.tick((tg, "t", k)))
                    if k:
                        j = k - 1
                        dve.wait_ge(*act_done.at((tg, "hi", j)))
                        for kind, c in KINDS[:cols_n // S]:
                            m = dve.scalar_tensor_tensor(xl[:, j, c], h_n[:, j % 3, c], mod[:, 2 * l + kind, tile0 + j:tile0 + j + 1],
                                                         xh[:, j, c].bitcast(F32), ALU.add, ALU.subtract)
                        m.then_inc(*dve_done.tick((tg, "lo", j)))

            def attend(tag, items, hook=lambda n: None, pre_y=lambda j: None):
                N = len(items)
                for n in range(N + 3):
                    if n < N:
                        hook(n)
                        it_ = items[n]
                        dve.wait_ge(*pe_done.at((tag, "s", n)))
                        b, b2 = score_banks(n)
                        if it_.get("bias") is not None:
                            c0, c1 = it_["bias_cols"]
                            dve.tensor_tensor(b[:, c0:c1], b[:, c0:c1], it_["bias"], ALU.add).then_inc(*dve_done.tick((tag, "biased", n)))
                            dve.wait_ge(*dve_done.at((tag, "biased", n)))
                        if n >= 4:
                            dve.wait_ge(*dve_done.at((tag, "y", n - 4)))
                        if it_.get("diff"):
                            dve.tensor_reduce(it_["st"](n, 0), b[:, 0:S], AX.X, ALU.max, negate=True)
                            dve.tensor_reduce(it_["st"](n, 1), b2[:, 0:S], AX.X, ALU.max, negate=True
                                              ).then_inc(*dve_done.tick((tag, "max", n)))
                        elif it_.get("sink") is not None:
                            dve.tensor_reduce(it_["st"](n, 0), b[:, 0:it_["nk"]], AX.X, ALU.max).then_inc(*dve_done.tick((tag, "m0", n)))
                            dve.wait_ge(*dve_done.at((tag, "m0", n)))
                            dve.tensor_scalar(it_["st"](n, 0), it_["st"](n, 0), it_["sink"], -1.0, ALU.max, ALU.mult
                                              ).then_inc(*dve_done.tick((tag, "max", n)))
                        else:
                            dve.tensor_reduce(it_["st"](n, 0), b[:, 0:it_["nk"]], AX.X, ALU.max, negate=True
                                              ).then_inc(*dve_done.tick((tag, "max", n)))
                    if 1 <= n <= N and items[n - 1].get("diff"):
                        j = n - 1
                        it_ = items[j]
                        dve.wait_ge(*act_done.at((tag, "exp", j)))
                        dve.reciprocal(it_["st2"](j, 2), it_["st2"](j, 2)).then_inc(*dve_done.tick((tag, "r", j)))
                        dve.wait_ge(*dve_done.at((tag, "r", j)))
                        if j >= 2:
                            dve.wait_ge(*pe_done.at((tag, "t", j - 2)))
                        dve.tensor_tensor(it_["st"](j, 3), it_["st"](j, 3), it_["neglam"], ALU.mult)
                        dve.tensor_scalar(it_["p"](j), it_["e"](j)[:, 0:S], it_["st"](j, 2), None, ALU.mult
                                          ).then_inc(*dve_done.tick((tag, "a0", j)))
                        dve.wait_ge(*dve_done.at((tag, "a0", j)))
                        dve.scalar_tensor_tensor(it_["p"](j), it_["e"](j)[:, S:2 * S], it_["st"](j, 3), it_["p"](j), ALU.mult, ALU.add
                                                 ).then_inc(*dve_done.tick((tag, "exp", j)))
                    if n >= 3:
                        j = n - 3
                        it_ = items[j]
                        pre_y(j)
                        if it_.get("diff"):
                            dve.wait_ge(*pe_done.at((tag, "o", j)))
                            dve.tensor_copy(it_["y"], out_at(it_["dv"])).then_inc(*dve_done.tick((tag, "y", j)))
                            continue
                        dve.wait_ge(*act_done.at((tag, "exp", j)))
                        if it_.get("sink") is not None:
                            dve.wait_ge(*act_done.at((tag, "sink", j)))
                            dve.tensor_tensor(it_["st"](j, 2), it_["st"](j, 2), it_["st"](j, 3), ALU.add
                                              ).then_inc(*dve_done.tick((tag, "den", j)))
                            dve.wait_ge(*dve_done.at((tag, "den", j)))
                        dve.reciprocal(it_["st"](j, 2), it_["st"](j, 2)).then_inc(*dve_done.tick((tag, "r", j)))
                        dve.wait_ge(*dve_done.at((tag, "r", j)))
                        dve.wait_ge(*pe_done.at((tag, "o", j)))
                        dve.tensor_scalar(it_["y"], out_at(64), it_["st"](j, 2), None, ALU.mult
                                          ).then_inc(*dve_done.tick((tag, "y", j)))

            def ffn(tag, p0, t0, last=False):
                def hidden(c, p, per, it, t, nstep, s_, turns):
                    step(p, per, it, turns)
                    dve.wait_ge(silu_done, it * nstep + (t + 1))
                    if t >= 2:
                        dve.wait_ge(hid_hi, it * nstep + (t - 1))
                    dve.tensor_tensor(hidf[:, c, :], sg[:, c, :], bank[4 + c][:, S:2 * S], ALU.mult).then_inc(hid_done, 1)
                    dve.wait_ge(hid_hi, it * nstep + (t + 1))
                    dve.tensor_tensor(hidl[:, s_, c, :], hidf[:, c, :], hidh[:, s_, c, :].bitcast(F32), ALU.subtract).then_inc(hid_lo, 1)

                def body(p, per, it, t, nstep, turns):
                    for half in range(2):
                        hidden(0, p + 3 * half, per, it, t + 2 * half, nstep, 1 - half, turns)
                        hidden(1, p + 1 + 3 * half, per, it, t + 1 + 2 * half, nstep, 1 - half, turns)
                        step(p + 2 + 3 * half, per, it, turns)
                hidden(0, p0, 0, 0, t0, 0, 0, 1)
                hidden(1, p0 + 1, 0, 0, t0 + 1, 0, 0, 1)
                n = 4 if last else 5
                with repeat(dve, n) as it:
                    body(p0 + 2, 6, it, t0 + 2, 4, n)
                if last:
                    body(p0 + 26, 0, 0, t0 + 18, 0, 1)
                step(p0 + 32)

            def turn_evac(tag, toks, write, n_tiles=4):
                for i, t in enumerate(toks):
                    for b in range(n_tiles // 4):
                        g = i * (n_tiles // 4) + b
                        dve.wait_ge(*pe_done.at((tag, "turn", g)))
                        write(i, b, bank[6 + g % 2].rearrange("p (c n) -> p c n", c=4)).then_inc(*dve_done.tick((tag, "turned", g)))

            site = [0]
            for l in range(L):
                stage(dve, "dve", ("mod", l), "load" if l == 0 else ("ffn", l - 1))
                p0 = base["mod", l]

                def mod_turn(p, per, it, turns, cols):
                    for j in range(3):
                        step(p + j, per, it, turns)
                        dve.wait_ge(panel_used, it * per + (p + j + 1))
                        dve.tensor_copy(modt[0:2, cols(j)], bank[5 + j][0:2, 0:S]).then_inc(mod_taken, 1)

                def mod_bias(tiles, part):
                    dve.wait_ge(*pe_done.at(("mod", l, "turn", part)))
                    o_ = PAR["b_mod"][0] + 48 * l
                    n0, n1 = tiles[0], tiles[-1] + 1
                    turned = bank[4][:, 0:96].rearrange("p (n v) -> p v n", v=2)
                    for v in range(2):
                        m = dve.tensor_tensor(mod[:, 2 * l + v, n0:n1], turned[:, v, n0:n1], par[:, o_ + n0:o_ + n1], ALU.add)
                    m.then_inc(*dve_done.tick(("mod", l, "vectors", part)))
                    dve.wait_ge(*dve_done.at(("mod", l, "vectors", part)))
                mod_turn(p0, 0, 0, 1, lambda j: slice(S * j, S * j + S))
                with repeat(dve, 7) as it:
                    mod_turn(p0 + 3, 3, it, 7, lambda j: bass.ds(it * (3 * S) + (3 + j) * S, S))
                mod_bias(range(16), 0)
                end("dve", ("mod", l))

                tg = ("norm1", l)
                stage(dve, "dve", tg, ("mod", l))
                mod_bias(range(16, 48), 1)
                modulated_norm(tg, l, 0, T)
                end("dve", tg)

                tg = ("mla", l)
                p0 = base["mla", l]
                stage(dve, "dve", tg, ("norm1", l))
                TM = mix_tokens(l)
                OT = TM // P
                g = 0
                for j, dsts, c in ((0, (0, 1), slice(0, TM)), (1, (3, 4), slice(0, T)), (2, (2,), slice(0, TM)), (3, (None,), slice(0, T))):
                    step(p0 + j)
                    for i, d_ in enumerate(dsts):
                        product(dve, tg, p0 + j, i, len(dsts), g)
                        b = bank[4 + g % 4]
                        if d_ is None:
                            m = dve.tensor_copy(kr[0:QH, :], b[0:QH, :])
                        else:
                            m = dve.tensor_copy(downs[:, d_, c], b[:, c])
                        m.then_inc(*dve_done.tick((tg, "ev", g)))
                        g += 1
                step(p0 + 4)
                dve.wait_ge(*pe_done.at((tg, "krot")))
                R = slice(NOPE, QH)
                c1, s1 = CONST["cos1"][0], CONST["sin1"][0]
                cos1, sin1 = cst[R, c1:c1 + S], cst[R, s1:s1 + S]

                def rope(dst, rot, label):
                    dve.tensor_tensor(rt[R, :], rot, sin1, ALU.mult)
                    dve.tensor_tensor(dst, dst, cos1, ALU.mult).then_inc(*dve_done.tick((label, "c")))
                    dve.wait_ge(*dve_done.at((label, "c")))
                    dve.tensor_tensor(dst, dst, rt[R, :], ALU.add).then_inc(*dve_done.tick(label))
                dve.wait_ge(*dve_done.at((tg, "ev", 5)))
                rope(kr[R, 0:S], bank[7][R, 0:S], (tg, "kr"))
                latents = (("q", 3, slice(0, TM), 0, qdh, qdl, "mla_q_norm_w", stat),
                           ("kv", 2, slice(0, T), 3, kvh, kvl, "mla_kv_norm_w", stat2))
                for name, n_, c_, off, hi_, lo_, w, st_ in latents:
                    t2 = (tg, name)
                    dve_rstd(dve, t2, c_, st_)
                    for k in range(n_):
                        dve.scalar_tensor_tensor(downs[:, off + k, c_], downs[:, off + k, c_], col(w, n_ * l + k), st_[:, c_],
                                                 ALU.mult, ALU.mult).then_inc(*dve_done.tick((t2, "t", k)))
                for name, n_, c_, off, hi_, lo_, w, st_ in latents:
                    for k in range(n_):
                        dve.wait_ge(*act_done.at(((tg, name), "hi", k)))
                        dve.tensor_tensor(lo_[:, k, c_], downs[:, off + k, c_], hi_[:, k, c_].bitcast(F32), ALU.subtract
                                          ).then_inc(*dve_done.tick(((tg, name), "lo", k)))
                dve_done.mark((tg, "lat ready"))
                for t in range(4):
                    dve.wait_ge(*pe_done.at((tg, "v", t)))
                    dve.tensor_copy(vtok[:, t, :], bank[t]).then_inc(*dve_done.tick((tg, "v", t)))
                raw_items = mla_items(l)
                per = len(raw_items) // HEADS

                def heads(hd):
                    if hd < HEADS - 1:
                        dve.wait_ge(*pe_done.at((tg, "qk", hd)))
                    else:
                        dve.wait_ge(panel_used, p0 + 7)
                    dve.tensor_copy(kt[0:64, hd % 2, :], bank[7][0:64, :]).then_inc(*dve_done.tick((tg, "kt", hd)))
                    dve.wait_ge(*act_done.at((tg, "q", hd)))
                    dve.wait_ge(*pe_done.at((tg, "rot", hd)))
                    rope(qt[R, hd % 2, 0:S], bank[6][R, 0:S], (tg, "qk", hd))
                heads(0)

                def hook(n):
                    if n % per == 1 and n // per + 1 < HEADS:
                        heads(n // per + 1)
                        if n // per + 1 == 4:
                            step(p0 + 5)
                items = [dict(nk=n_, dv=64, y=ytok[:, q, 64 * hd:64 * hd + 64],
                              st=lambda j, c: st8[:, 4 * (j % 4) + c:4 * (j % 4) + c + 1]) for hd, q, _, n_ in raw_items]
                attend(tg, items, hook)
                step(p0 + 6)
                for i in range(OT):
                    dve_done.mark(((tg, "y"), "ready", i))
                turn_evac((tg, "y"), range(OT), lambda i, b, src: dve.tensor_copy(y[:, 0:4, P * i:P * i + P], src))
                end("dve", tg)

                tg = ("gla", l)
                p0 = base["gla", l]
                stage(dve, "dve", tg, ("mla", l))
                g = 0
                for j in range(5):
                    step(p0 + j)
                    n = (2, 2, 4, 4, 1)[j]
                    for i in range(n):
                        product(dve, tg, p0 + j, i, n, g)
                        b = bank[4 + g % 4]
                        if j == 0:
                            m = dve.tensor_scalar(gq[:, i, :], b, 64 ** -0.5, None, ALU.mult)
                        elif j == 1:
                            m = dve.tensor_copy(gk[:, i, :], b)
                        elif j < 4:
                            m = dve.tensor_copy(gv[:, i, 256 * (j - 2):256 * (j - 2) + 256], b[:, 0:256])
                        else:
                            m = dve.tensor_copy(lr[0:32, :], b[0:32, :])
                        m.then_inc(*dve_done.tick((tg, "ev", g)))
                        g += 1
                for t in range(4):
                    zb = bank[4 + t % 2]
                    dve.wait_ge(*pe_done.at((tg, "z", t)))
                    dve.tensor_scalar(la[:, t, :], zb, 0.0, None, ALU.min).then_inc(*dve_done.tick((tg, "zmin", t)))
                    dve.wait_ge(*dve_done.at((tg, "zmin", t)))
                    dve.scalar_tensor_tensor(ez[:, t, :], la[:, t, :], 2.0, zb, ALU.mult, ALU.subtract).then_inc(*dve_done.tick((tg, "negabs", t)))
                    dve.wait_ge(*pe_done.at((tg, "ktok", t)))
                    dve.tensor_copy(ktok[:, t, :], bank[6 + t % 2][:, 0:S]).then_inc(*dve_done.tick((tg, "ktok", t)))
                for t in range(4):
                    dve.wait_ge(*act_done.at((tg, "ln", t)))
                    dve.tensor_tensor(la[:, t, :], la[:, t, :], ez[:, t, :], ALU.subtract).then_inc(*dve_done.tick((tg, "la", t)))
                for d, dn in enumerate("fb"):
                    dt_ = (tg, dn)
                    if d:
                        dve.wait_ge(*pe_done.at(((tg, "f"), "from state", 7)))
                    else:
                        dve.wait_ge(*dve_done.at((tg, "la", 3)))
                    dve.memset(attm[:], 0.0).then_inc(*dve_done.tick((dt_, "zero")))
                    dve.memset(state[:], 0.0).then_inc(*dve_done.tick((dt_, "state", -1)))
                    for f in range(2):
                        dve.wait_ge(*act_done.at((dt_, "expp", f)))
                        dve.tensor_tensor(qdec[:, f, :], gq[:, f, :], expc[:, f, :], ALU.mult)
                        dve.wait_ge(*act_done.at((dt_, "expn", f)))
                        m = dve.tensor_tensor(kinv[:, f, :], gk[:, f, :], kinv[:, f, :], ALU.mult)
                    m.then_inc(*dve_done.tick((dt_, "kinv")))
                    for t in range(4):
                        dve.wait_ge(*act_done.at((dt_, "rem", t)))
                        dve.tensor_tensor(kend[:, t, :], kend[:, t, :], ktok[:, t, :], ALU.mult).then_inc(*dve_done.tick((dt_, "kend", t)))
                    mask = const("tri_" + dn).bitcast(I32).unsqueeze(1).broadcast_to([P, 2, P])
                    dve.wait_ge(*dve_done.at((dt_, "state", -1)))
                    for t in range(OT):
                        dve.wait_ge(*pe_done.at((dt_, "att", t)))
                        if t >= 2:
                            dve.wait_ge(*pe_done.at((dt_, "intra", t - 2)))
                        for b in range(2):
                            m = dve.copy_predicated(attm[:, t % 2, :].rearrange("p (f b n) -> p f b n", f=2, b=2)[:, :, b, :], mask,
                                                    bank[4 + 2 * (t % 2) + b][:, 0:S].rearrange("p (f n) -> p f n", f=2))
                        m.then_inc(*dve_done.tick((dt_, "att", t)))
                    order = [4, 5, 6, 7, 0, 1, 2, 3] if d == 0 else [7, 6, 5, 4, 3, 2, 1, 0]
                    for n, chunk in enumerate(order):
                        c_ = 64 * chunk + (63 if d == 0 else 0)
                        if n == 7:
                            break
                        dve.wait_ge(*pe_done.at((dt_, "kv", n)))
                        if n >= 2:
                            dve.wait_ge(*pe_done.at((dt_, "from state", n - 1)))
                        for f in range(2):
                            for b in range(2):
                                q = slice(64 * b, 64 * b + 64)
                                m = dve.scalar_tensor_tensor(state[q, (n + 1) % 2, f, P * b:P * b + P], state[q, n % 2, f, P * b:P * b + P],
                                                             expc[q, f, c_:c_ + 1], bank[4 + n % 2][q, P * f:P * f + P], ALU.mult, ALU.add)
                        m.then_inc(*dve_done.tick((dt_, "state", n)))
                        dve.wait_ge(*dve_done.at((dt_, "state", n)))
                    dve_done.mark((dt_, "end"))
                dve.wait_ge(*act_done.at((tg, "gstd")))
                dve.reciprocal(gst[:, 0:4 * OT], gst[:, 0:4 * OT]).then_inc(*dve_done.tick((tg, "grstd")))
                dve.wait_ge(*dve_done.at((tg, "grstd")))
                for i in range(OT):
                    for hd in range(4):
                        m = dve.scalar_tensor_tensor(gv[:, i, P * hd:P * hd + P], bank[i][:, P * hd:P * hd + P],
                                                     gst[:, 4 * i + hd:4 * i + hd + 1], gln[:, l, :], ALU.mult, ALU.mult)
                    m.then_inc(*dve_done.tick((tg, "gn", i)))
                    dve.wait_ge(*dve_done.at((tg, "gn", i)))
                    dve.wait_ge(*act_done.at((tg, "silu", i)))
                    dve.tensor_tensor(gv[:, i, :], gv[:, i, :], la[:, i, :], ALU.mult).then_inc(*dve_done.tick(((tg, "y"), "ready", i)))
                turn_evac((tg, "y"), range(OT), lambda i, b, src: dve.tensor_copy(y[:, 4:8, P * i:P * i + P], src))
                step(p0 + 5)
                step(p0 + 6)
                end("dve", tg)

                tg = ("na", l)
                p0 = base["na", l]
                stage(dve, "dve", tg, ("gla", l))
                g = 0
                for j in range(6):
                    step(p0 + j)
                    n = 2 if j < 4 else 4
                    for i in range(n):
                        product(dve, tg, p0 + j, i, n, g)
                        b = bank[4 + g % 4]
                        if j < 2:
                            m = dve.tensor_scalar(nq[:, 2 * j + i, 0:TM], b[:, 0:TM], HD ** -0.5, None, ALU.mult)
                        elif j < 4:
                            m = dve.tensor_copy(nk[:, 2 * (j - 2) + i, :], b)
                        else:
                            m = dve.tensor_copy(nv[:, i, 256 * (j - 4):256 * (j - 4) + 256], b[:, 0:256])
                        m.then_inc(*dve_done.tick((tg, "ev", g)))
                        g += 1
                na_list = sorted(raw_items, key=lambda x: (x[1], x[0]))
                dve.wait_ge(*pool_done.at((tg, "bias", 1)))
                items = [dict(nk=n_, dv=64, y=nytok[:, 0, 64 * hd:64 * hd + 64],
                              bias=nbias[:, hd, 2 - 2 * q:6 - 2 * q, :] if q < 2 else None, bias_cols=(0, S),
                              st=lambda j, c: nst[:, 4 * (j % 4) + c:4 * (j % 4) + c + 1]) for hd, q, _, n_ in na_list]
                for i_ in items:
                    if i_["bias"] is not None:
                        i_["bias"] = i_["bias"].rearrange("p a b -> p (a b)")

                def pre_y(j):
                    if j % HEADS == 0 and j:
                        dve.wait_ge(*pe_done.at((tg, "turn", j // HEADS - 1)))
                attend(tg, items, pre_y=pre_y)
                end("dve", tg)

                tg = ("merge", l)
                p0 = base["merge", l]
                stage(dve, "dve", tg, ("na", l))
                for k in range(12):
                    dve.wait_ge(*act_done.at((tg, "yh", k)))
                    dve.tensor_tensor(yl[:, k, 0:TM], y[:, k, 0:TM], yh[:, k, 0:TM].bitcast(F32), ALU.subtract
                                      ).then_inc(*dve_done.tick((tg, "yl") if k == 11 else None))
                c = slice(0, TM)
                with repeat(dve, 8) as it:
                    step(p0, 3, it, 8)
                    step(p0 + 1, 3, it, 8)
                    dve.wait_ge(gate_ready, it * 3 + (24 * l + 3))
                    dve.wait_ge(panel_used, it * 3 + (p0 + 2))
                    dve.tensor_tensor(mt[:, 0, c], gates[:, 0, c], bank[3][:, c], ALU.mult)
                    dve.tensor_tensor(mt[:, 1, c], gates[:, 1, c], bank[4][:, c], ALU.mult).then_inc(*dve_done.tick((tg, "ab")))
                    step(p0 + 2, 3, it, 8)
                    dve.wait_ge(panel_used, it * 3 + (p0 + 3))
                    dve.tensor_tensor(mt[:, 2, c], gates[:, 2, c], bank[5][:, c], ALU.mult)
                    dve.wait_ge(*dve_done.at((tg, "ab"), it))
                    dve.tensor_tensor(mt[:, 0, c], mt[:, 0, c], mt[:, 1, c], ALU.add).then_inc(*dve_done.tick((tg, "abc")))
                    dve.wait_ge(*dve_done.at((tg, "abc"), it))
                    dve.tensor_tensor(mf[:, bass.ds(it, 1), c], mt[:, 0:1, c], mt[:, 2:3, c], ALU.add).then_inc(merged, 1)
                end("dve", tg)

                tg = ("out", l)
                stage(dve, "dve", tg, ("merge", l))
                for k in range(8):
                    dve.wait_ge(*act_done.at((tg, "mh", k)))
                    dve.tensor_tensor(xl[:, k, c], mf[:, k, c], xh[:, k, c].bitcast(F32), ALU.subtract
                                      ).then_inc(*dve_done.tick((tg, "ml") if k == 7 else None))
                for j in range(4):
                    step(base[tg] + j)
                    for i in range(2):
                        g = 2 * j + i
                        product(dve, tg, base[tg] + j, i, 2, g)
                        for kind, cc in KINDS[:TM // S]:
                            m = dve.scalar_tensor_tensor(h[:, g, cc], bank[4 + g % 4][:, cc], mod[:, 2 * l + kind, 16 + g:17 + g],
                                                         h[:, g, cc], ALU.mult, ALU.add)
                        m.then_inc(*dve_done.tick((tg, "ev", g)))
                end("dve", tg)

                tg = ("norm2", l)
                stage(dve, "dve", tg, ("out", l))
                modulated_norm(tg, l, 24, TM)
                end("dve", tg)
                for part in range(TM // S):
                    tg = ("ffn", l, part)
                    stage(dve, "dve", tg, ("norm2", l) if part == 0 else ("ffn", l, part - 1))
                    ffn(tg, base[tg], FT * site[0])
                    site[0] += 1
                    dve.wait_ge(panel_used, base[tg] + 33)
                    for k in range(8):
                        cc = KINDS[part][1]
                        dve.scalar_tensor_tensor(h[:, k, cc], bank[k // 2][:, S * (k % 2):S * (k % 2) + S],
                                                 mod[:, 2 * l + part, 40 + k:41 + k], h[:, k, cc], ALU.mult, ALU.add
                                                 ).then_inc(*dve_done.tick((tg, "h", k)))
                    end("dve", tg)
                end("dve", ("ffn", l))

            stage(dve, "dve", "block2", ("ffn", L - 1))
            dve_rstd(dve, "final", slice(0, S))
            for k in range(9):
                if k < 8:
                    dve.scalar_tensor_tensor(h[:, k, 0:S], h[:, k, 0:S], col("final_norm_w", k), stat[:, 0:S], ALU.mult, ALU.mult
                                             ).then_inc(*dve_done.tick(("final", "t", k)))
                if k:
                    dve.wait_ge(*act_done.at(("final", "hi", k - 1)))
                    dve.tensor_tensor(xl[:, k - 1, 0:S], h[:, k - 1, 0:S], xh[:, k - 1, 0:S].bitcast(F32), ALU.subtract
                                      ).then_inc(*dve_done.tick(("final", "lo", k - 1)))
            dve.wait_ge(*loaded2.at("block2"))
            dve.tensor_copy(ang[:, 2, :], pos[:]).then_inc(*dve_done.tick("posf"))
            dve.wait_ge(*dve_done.at("posf"))
            dve.tensor_scalar(ang[:, 2, :], ang[:, 2, :], const2("inv"), None, ALU.mult).then_inc(*dve_done.tick("ang"))
            dve.wait_ge(*dve_done.at("ang"))
            TWO_PI = 2 * math.pi
            P1 = 6.28125
            P2 = float(np.float32(np.round((TWO_PI - P1) * 2 ** 21) / 2 ** 21))
            P3 = float(np.float32(TWO_PI - P1 - P2))
            MAGIC = float(1.5 * 2 ** 23)
            PI = float(np.nextafter(np.float32(math.pi), np.float32(0)))
            for n in range(2):
                dve.tensor_scalar(rtmp[:, 1, :], ang[:, 2, :], 1.0 / TWO_PI, 0.25 * n, ALU.mult, ALU.add).then_inc(*dve_done.tick(("u", n)))
                dve.wait_ge(*dve_done.at(("u", n)))
                dve.tensor_scalar(rtmp[:, 1, :], rtmp[:, 1, :], MAGIC, MAGIC, ALU.add, ALU.subtract).then_inc(*dve_done.tick(("turns", n)))
                dve.wait_ge(*dve_done.at(("turns", n)))
                src = ang[:, 2, :]
                for i, c_ in enumerate((P1, P2, P3)):
                    dve.scalar_tensor_tensor(ang[:, n, :], rtmp[:, 1, :], -c_, src, ALU.mult, ALU.add).then_inc(*dve_done.tick(("less", n, i)))
                    dve.wait_ge(*dve_done.at(("less", n, i)))
                    src = ang[:, n, :]
                dve.tensor_scalar(ang[:, n, :], ang[:, n, :], n * math.pi / 2, PI, ALU.add, ALU.min).then_inc(*dve_done.tick(("clip", n)))
                dve.wait_ge(*dve_done.at(("clip", n)))
                dve.tensor_scalar(ang[:, n, :], ang[:, n, :], -PI, None, ALU.max).then_inc(*dve_done.tick(("angle", n)))
            def ltmp(l, c_):
                return rtmp[:, (2 * l + c_) // 4, 64 * ((2 * l + c_) % 4):64 * ((2 * l + c_) % 4) + 64]
            for l in range(L):
                for c_ in range(2):
                    dve.tensor_tensor(ltmp(l, c_), lamv[:, l, 2 * c_, :], lamv[:, l, 2 * c_ + 1, :], ALU.mult
                                      ).then_inc(*dve_done.tick(("lam", l, c_)))
                    dve.wait_ge(*dve_done.at(("lam", l, c_)))
                    dve.tensor_reduce(ast[:, 2 * l + c_:2 * l + c_ + 1], ltmp(l, c_), AX.X, ALU.add
                                      ).then_inc(*dve_done.tick("lam dots" if (l, c_) == (L - 1, 1) else None))
            dve.wait_ge(*act_done.at("lam exp"))
            for l in range(L):
                lambda_init = 0.8 - 0.6 * math.exp(-0.3 * l)
                dve.scalar_tensor_tensor(lam[:, l:l + 1], ast[:, 2 * l + 1:2 * l + 2], -lambda_init, ast[:, 2 * l:2 * l + 1],
                                         ALU.add, ALU.subtract)
                dve.tensor_scalar(subln[:, l, :], subln[:, l, :], 1.0 - lambda_init, None, ALU.mult).then_inc(*dve_done.tick(("lam", l)))
            end("dve", "block2")
            prev = "block2"

            def layer_norm_dve(tg, last=False):
                dve.wait_ge(*act_done.at((tg, "mean")))
                for k in range(8):
                    dve.tensor_tensor(h[:, k, 0:S], h[:, k, 0:S], rtmp[:, 0, :], ALU.subtract).then_inc(*dve_done.tick((tg, "d", k)))
                dve_rstd(dve, tg, slice(0, S))
                for k in range(9):
                    if k < 8:
                        dve.scalar_tensor_tensor(h[:, k, 0:S], h[:, k, 0:S], col("ln_g_2", ln_col(tg) + k), stat[:, 0:S], ALU.mult, ALU.mult
                                                 ).then_inc(*dve_done.tick((tg, "t", k)))
                    if k and not last:
                        j = k - 1
                        dve.wait_ge(*act_done.at((tg, "hi", j)))
                        dve.scalar_tensor_tensor(xl[:, j, 0:S], h[:, j, 0:S], col("ln_b_2", ln_col(tg) + j), xh[:, j, 0:S].bitcast(F32),
                                                 ALU.add, ALU.subtract).then_inc(*dve_done.tick((tg, "lo", j)))

            for l in range(L):
                for which in (1, 2):
                    if which == 2:
                        tg = ("win2", l)
                        p0 = base[tg]
                        stage(dve, "dve", tg, prev)
                        g = 0
                        for j in range(9):
                            step(p0 + j)
                            n = 3 if j == 8 else 2
                            for i in range(n):
                                product(dve, tg, p0 + j, i, n, g)
                                b = bank[4 + g % 4]
                                if j < 4:
                                    dst, src, sc = f2[:, 2 * j + i, :], b[:, 0:S], HD ** -0.5 if j < 2 else 1.0
                                elif j < 6:
                                    dst, src, sc = dvt[:, i, 256 * (j - 4):256 * (j - 4) + 256], b[:, 0:S], 1.0
                                elif j < 8:
                                    dst, src, sc = f2[:, 8 + 2 * (j - 6) + i, :], b[:, 0:S], HD ** -0.5
                                elif i == 0:
                                    dst, src, sc = f2[:, 12, :], b[:, 0:S], 1.0
                                else:
                                    dst, src, sc = dvt[:, i - 1, 512:640], b[:, 0:P], 1.0
                                dve.tensor_scalar(dst, src, sc, None, ALU.mult).then_inc(*dve_done.tick((tg, "ev", g)))
                                g += 1
                        for i in range(13):
                            dve.wait_ge(*pe_done.at((tg, "rot", i)))
                            dve.tensor_tensor(rtmp[:, i % 2, :], bank[i % 2][:, 0:S], sin2[:], ALU.mult)
                            dve.tensor_tensor(f2[:, i, :], f2[:, i, :], cos2[:], ALU.mult).then_inc(*dve_done.tick((tg, "cos", i)))
                            dve.wait_ge(*dve_done.at((tg, "cos", i)))
                            dve.tensor_tensor(f2[:, i, :], f2[:, i, :], rtmp[:, i % 2, :], ALU.add).then_inc(*dve_done.tick((tg, "roped", i)))
                        dve.wait_ge(*pe_done.at((tg, "swap")))
                        dve.tensor_copy(f2[:, 13, :], bank[2][:, 0:S]).then_inc(*dve_done.tick((tg, "swap")))
                        end("dve", tg)
                        tg = ("att2", l)
                        stage(dve, "dve", tg, ("win2", l))

                        def st(j, c):
                            return ast[:, 4 * (j % 4) + c:4 * (j % 4) + c + 1]

                        def st2(j, c):
                            return ast[:, 4 * (j % 4) + c:4 * (j % 4) + c + 2]
                        o_ = CONST["band"][0] - N_CONST1
                        items = [dict(nk=S, dv=P, diff=True, st=st, st2=st2, neglam=lam[:, l:l + 1], e=prd,
                                      p=lambda j: ap_[:, j % 2, 0:S], y=ytok2[:, q, P * hd:P * hd + P])
                                 for hd in range(4) for q in range(2)]
                        items += [dict(nk=S, dv=64, st=st, sink=sink[:, l, hd:hd + 1], bias=cst2[:, o_ + S * q:o_ + S * q + S],
                                       bias_cols=(0, S), y=ytok2[:, q, 512 + 64 * hd:576 + 64 * hd])
                                  for hd in range(8) for q in range(2)]
                        attend(tg, items)
                        dve.wait_ge(*act_done.at((tg, "std")))
                        dve.reciprocal(ast[:, 16:24], ast[:, 16:24]).then_inc(*dve_done.tick((tg, "rstd")))
                        dve.wait_ge(*dve_done.at((tg, "rstd")))
                        for i in range(2):
                            for hd in range(4):
                                v = ytok2[:, i, P * hd:P * hd + P]
                                m = dve.scalar_tensor_tensor(v, v, ast[:, 16 + 4 * i + hd:17 + 4 * i + hd], subln[:, l, :], ALU.mult, ALU.mult)
                            m.then_inc(*dve_done.tick(((tg, "y"), "ready", i)))

                        def write(i, b, src):
                            dve.wait_ge(*act_done.at((tg, "turned hi", 2 * i + b)))
                            dst = slice(4 * b, 4 * b + 4)
                            return dve.tensor_tensor(xl[:, dst, P * i:P * i + P], src, xh[:, dst, P * i:P * i + P].bitcast(F32), ALU.subtract)
                        turn_evac((tg, "y"), range(2), write, n_tiles=8)
                        end("dve", tg)
                        tg = ("out2", l)
                        stage(dve, "dve", tg, ("att2", l))
                        dve_done.mark((tg, "ml"))
                        dve.wait_ge(*pool_done.at((("ffn1", l), "h", 7)))
                        for j in range(4):
                            step(base[tg] + j)
                            for i in range(2):
                                g = 2 * j + i
                                product(dve, tg, base[tg] + j, i, 2, g)
                                dve.scalar_tensor_tensor(h[:, g, 0:S], h[:, g, 0:S], ALPHA, bank[4 + g % 4][:, 0:S], ALU.mult, ALU.add
                                                         ).then_inc(*dve_done.tick((tg, "u", g)))
                                dve_done.mark((tg, "ev", g))
                        layer_norm_dve(tg)
                        end("dve", tg)
                        prev = tg
                    tg = ("ffn%d" % which, l)
                    stage(dve, "dve", tg, prev)
                    last = which == 2 and l == L - 1
                    ffn(tg, base[tg], FT * site[0], last)
                    site[0] += 1
                    dve.wait_ge(panel_used, base[tg] + 33)
                    if prev != "block2":
                        dve.wait_ge(*pool_done.at((prev, "h", 7)))
                    for k in range(8):
                        dve.scalar_tensor_tensor(h[:, k, 0:S], h[:, k, 0:S], 2 * ALPHA, bank[k // 2][:, S * (k % 2):S * (k % 2) + S],
                                                 ALU.mult, ALU.add).then_inc(*dve_done.tick((tg, "u", k)))
                    layer_norm_dve(tg, last)
                    end("dve", tg)
                    prev = tg
            stage(dve, "dve", "store", prev)
            for g in (0, 2, 1, 3):
                dve.wait_ge(*pe_done.at(("oT", g)))
                dve.tensor_copy(ytok2[:, g // 2, 512 * (g % 2):512 * (g % 2) + 512], bank[g]).then_inc(*dve_done.tick(("stored", g)))
            end("dve", "store")

        @block.gpsimd
        def _(pool):
            def step(p, per=0, it=0, turns=1):
                split_pool(pool, p + 2, per, it, turns)

            pool.memset(ones[:], 1.0)
            pool.memset(eps[:, 0:1], EPS1)
            pool.memset(eps[:, 1:2], EPS2)
            pool.memset(eps[:, 2:3], 4 * EPS2)
            pool.memset(wg[:], 0.0)
            pool.memset(zero[:], 0.0).then_inc(*pool_done.tick("setup"))
            end("pool", "load")
            split_pool(pool, 0)
            split_pool(pool, 1)

            def layer_norm_pool(tg):
                for k in range(8):
                    pool.wait_ge(*dve_done.at((tg, "lo", k)))
                    pool.tensor_scalar(h[:, k, 0:S], h[:, k, 0:S], col("ln_b_2", ln_col(tg) + k), None, ALU.add
                                       ).then_inc(*pool_done.tick((tg, "h", k)))

            def ffn(tag, p0, last=False, norm=None):
                for j in range(2):
                    step(p0 + j)
                if norm is not None:
                    layer_norm_pool(norm)
                n = 4 if last else 5
                with repeat(pool, n) as it:
                    for j in range(6):
                        step(p0 + 2 + j, 6, it, n)
                if last:
                    for j in range(6):
                        step(p0 + 26 + j)
                step(p0 + 32)

            for l in range(L):
                p0 = base["mod", l]
                for j in range(3):
                    step(p0 + j)
                with repeat(pool, 7) as it:
                    for j in range(3):
                        step(p0 + 3 + j, 3, it, 7)
                end("pool", ("mod", l))
                end("pool", ("norm1", l))
                tg = ("mla", l)
                p0 = base["mla", l]
                stage(pool, "pool", tg, ("norm1", l))
                for j in range(5):
                    step(p0 + j)
                pool.wait_ge(*dve_done.at((tg, "kr")))
                for hd in range(HEADS):
                    if hd < HEADS - 1:
                        pool.wait_ge(*pe_done.at((tg, "qk", hd)))
                    else:
                        pool.wait_ge(panel_used, p0 + 7)
                    if hd in (0, 5):
                        pool.wait_ge(lo_ready_pool, p0 + (8 if hd else 7))
                    pool.tensor_copy(kt[NOPE:QH, hd % 2, :], kr[NOPE:QH, :]).then_inc(*pool_done.tick((tg, "krcopy", hd)))
                    pool.wait_ge(*pool_done.at((tg, "krcopy", hd)))
                    if hd == 4:
                        step(p0 + 5)
                step(p0 + 6)
                end("pool", tg)
                tg = ("gla", l)
                p0 = base["gla", l]
                stage(pool, "pool", tg, ("mla", l))
                pool.wait_ge(lo_ready_pool, p0 + 2)
                pool.memset(lr[32:33, :], 1.0).then_inc(*pool_done.tick((tg, "ones")))
                pool.wait_ge(*pool_done.at((tg, "ones")))
                for j in range(7):
                    step(p0 + j)
                end("pool", tg)
                tg = ("na", l)
                p0 = base["na", l]
                stage(pool, "pool", tg, ("gla", l))
                pool.wait_ge(*bias_loaded.at(("bias", l)))
                pool.wait_ge(lo_ready_pool, p0 + 2)
                for r in range(2):
                    b = nbias[64 * r:64 * r + 64].rearrange("p h s c -> p (h s) c")
                    pool.affine_select(b[:, :, 0:48], b[:, :, 0:48], pattern=[[0, 48], [1, 48]], compare_op=ALU.is_ge, fill=NEG,
                                       base=8, channel_multiplier=-1).then_inc(*pool_done.tick((tg, "low", r)))
                    pool.wait_ge(*pool_done.at((tg, "low", r)))
                    pool.affine_select(b[:, :, 16:64], b[:, :, 16:64], pattern=[[0, 48], [-1, 48]], compare_op=ALU.is_ge, fill=NEG,
                                       base=-9, channel_multiplier=1).then_inc(*pool_done.tick((tg, "bias", r)))
                    pool.wait_ge(*pool_done.at((tg, "bias", r)))
                for j in range(6):
                    step(p0 + j)
                end("pool", tg)
                p0 = base["merge", l]
                with repeat(pool, 8) as it:
                    for j in range(3):
                        step(p0 + j, 3, it, 8)
                end("pool", ("merge", l))
                for j in range(4):
                    step(base["out", l] + j)
                end("pool", ("out", l))
                end("pool", ("norm2", l))
                for part in range(mix_tokens(l) // S):
                    ffn(("ffn", l, part), base["ffn", l, part])
                    end("pool", ("ffn", l, part))
                end("pool", ("ffn", l))
            end("pool", "block2")

            prev = None
            for l in range(L):
                for which in (1, 2):
                    if which == 2:
                        for j in range(9):
                            step(base["win2", l] + j)
                            if j == 1:
                                layer_norm_pool(prev)
                        end("pool", ("win2", l))
                        end("pool", ("att2", l))
                        for j in range(4):
                            step(base["out2", l] + j)
                        end("pool", ("out2", l))
                        prev = ("out2", l)
                    tg = ("ffn%d" % which, l)
                    ffn(tg, base[tg], last=which == 2 and l == L - 1, norm=prev)
                    end("pool", tg)
                    prev = tg
            end("pool", "store")

        @block.sync
        def _(sp):
            def row(v):
                return v.unsqueeze(0)

            for t in range(4):
                src = a["x"][0] if t < 2 else a["ctx"][0]
                sp.dma_start(xtok[:, t, :], src[P * (t % 2):P * (t % 2) + P, :]).then_inc(*loaded.tick(None, 16))
            for j, names in enumerate(PAR_TILES):
                r0 = 0
                for name in names:
                    n = PAR[name][1]
                    src = a[name]
                    nd = len(src.shape)
                    if nd == 3:
                        src = src.rearrange("a b c -> (a b c)")
                    elif nd == 2:
                        src = src.rearrange("a b -> (a b)")
                    sp.dma_start(ptok[r0:r0 + n, j, :], src.rearrange("(r p) -> r p", p=P)).then_inc(*loaded.tick(None, 16))
                    r0 += n
            sp.dma_start(cst[:], a["constants"][:, 0:N_CONST1]).then_inc(*loaded.tick(None, 16))
            for l in range(L):
                sp.dma_start(gln[:, l, :], row(a["gla_norm_w"][l]).broadcast_to([P, P])).then_inc(*loaded.tick(None, 16))
            loaded.mark("inputs")

            def wg_loads(l):
                sp.wait_ge(*pool_done.at("setup"))
                if l:
                    sp.wait_ge(*pe_done.at((("gla", l - 1), "z", 3)))
                for r, c, name in ((0, 0, "gla_w_gate_f"), (16, 256, "gla_w_gate_b")):
                    sp.dma_start(wg[r:r + 16, c:c + 256], a[name][l]).then_inc(*loaded2.tick(None, 16))
                for c, name in ((0, "gla_b_gate_f"), (256, "gla_b_gate_b")):
                    sp.dma_start(wg[32:33, c:c + 256], row(a[name][l])).then_inc(*loaded2.tick(None, 16))
                loaded2.mark(("wg", l))

            def band_writes(l):
                rpb = a["na_rpb"]
                n_r, n_c = 2 * NA_KH - 1, 2 * NA_KW - 1
                for d in range(7):
                    off = l * HEADS * n_r * n_c + (d - 3 + NA_KH - 1) * n_c + NA_KW - 1
                    src = bass.AP(rpb.tensor, rpb.offset + off, [[n_r * n_c, HEADS], [-1, 64], [1, 64]])
                    sp.dma_start(bands[l, d], src).then_inc(*bands_written.tick(None, 16))
                bands_written.mark(("bands", l))

            def bias_loads(l):
                for s_ in (pe_done, act_done, dve_done, pool_done):
                    sp.wait_ge(*s_.at(("end", ("gla", l))))
                sp.wait_ge(*bands_written.at(("bands", l)))
                for r in range(2):
                    for s_ in range(6):
                        src = bands[l, s_ + 1 - r].rearrange("h p c -> p h c")
                        sp.dma_start(nbias[64 * r:64 * r + 64, :, s_, :], src).then_inc(*bias_loaded.tick(None, 16))
                bias_loaded.mark(("bias", l))

            def block2_loads():
                sp.wait_ge(*dve_done.at((("out", L - 1), "ml")))
                sp.dma_start(cst2[:], a["constants"][:, N_CONST1:N_CONST]).then_inc(*loaded2.tick(None, 16))
                sp.dma_start(pos[:], a["positions_2"].broadcast_to([P, S])).then_inc(*loaded2.tick(None, 16))
                for dst, name in ((subln, "diff_subln_g_2"), (sink, "swa_sink_2"), (lamv, "diff_lambda_2")):
                    for l in range(L):
                        src = a[name][l]
                        n = int(np.prod(src.shape))
                        if len(src.shape) == 2:
                            src = src.rearrange("a b -> (a b)")
                        d = dst[:, l] if len(dst[:, l].shape) == 2 else dst[:, l].rearrange("p a b -> p (a b)")
                        sp.dma_start(d, row(src).broadcast_to([P, n])).then_inc(*loaded2.tick(None, 16))
                loaded2.mark("block2")

            before = {base["mla", l]: [lambda l=l: wg_loads(l), lambda l=l: band_writes(l)] for l in range(L)}
            for l in range(L):
                before[base["na", l] + 5] = [lambda l=l: bias_loads(l)]
            before[base["ffn", L - 1, 0] + 1] = [block2_loads]
            with nc.allow_non_contiguous_dma("diagonals of the bias table and broadcast rows"):
                for turns, first, panels in segments:
                    if turns > 1:
                        with repeat(sp, turns) as it:
                            for j, (_, parts) in enumerate(panels):
                                load_panel(sp, parts, first + j, len(panels), it)
                    else:
                        for j, (_, parts) in enumerate(panels):
                            for f_ in before.get(first + j, ()):
                                f_()
                            load_panel(sp, parts, first + j, 0, 0)
            for g in range(2):
                sp.wait_ge(*dve_done.at(("stored", 2 * g + 1)))
                sp.dma_start(out[0, P * g:P * g + P, :], ytok2[:, g, :]).then_inc(*stored.tick("out", 16))
            sp.wait_ge(*stored.at("out"))
    return {n: s.marks for n, s in signals.items()}


INPUTS = ("x", "c", "ctx", "c_ctx", "w_mod", "b_mod", "norm1_w", "w_in", "mla_q_norm_w", "mla_kv_norm_w",
          "mla_w_q_up", "mla_w_kv_up", "gla_w_gate_f", "gla_b_gate_f", "gla_w_gate_b", "gla_b_gate_b", "gla_norm_w",
          "na_rpb", "w_a_o", "w_b_o", "w_c_o", "w_out", "norm2_w", "w_ffn_in", "w_ffn_out", "final_norm_w",
          "positions_2", "w_in_2", "w_out_2", "diff_lambda_2", "diff_subln_g_2", "swa_sink_2", "ffn1_w_in_2",
          "ffn1_w_out_2", "ffn2_w_in_2", "ffn2_w_out_2", "ln_g_2", "ln_b_2")


def kernel(**inputs):
    import concourse.bacc as bacc
    from concourse.bass_utils import run_bass_kernel_spmd

    arrays = {f"in_{n}": np.ascontiguousarray(inputs[n]) for n in INPUTS}
    arrays["in_constants"] = constants()

    def build(known):
        nc = bacc.Bacc("TRN2", target_bir_lowering=False, num_devices=1)
        a = {n[3:]: nc.dram_tensor(n, v.shape, mybir.dt.from_np(v.dtype), kind="ExternalInput").ap()
             for n, v in arrays.items()}
        out = nc.dram_tensor("out", (1, S, D), F32, kind="ExternalOutput").ap()
        return nc, program(nc, a, out, known)

    _, known = build(None)
    nc, _ = build(known)
    return run_bass_kernel_spmd(nc, [arrays], core_ids=[0]).results[0]["out"]
```
